# Optimizing a Trainium2 kernel written in Bass

```python
import jax
import jax.numpy as jnp
from jax import lax
import numpy as np
import math
import jax, jax.numpy as jnp

D_MODEL = 1024
BATCH = 1
SEQ = 512
DEPTH = 1

HEAD_DIM = 64
RWKV_WIDTH = D_MODEL // 2
RWKV_HEADS = RWKV_WIDTH // HEAD_DIM
DECAY_LORA = 64
ICLR_LORA = 64
RWKV_GN_EPS = 64e-5
NSA_WIDTH = D_MODEL // 4
NSA_HEADS = NSA_WIDTH // HEAD_DIM
N_BRANCH = 3
CMP_BLOCK = 32
CMP_STRIDE = 16
SEL_BLOCK = 64
SEL_TOPK = 16
WINDOW = 512
MEM_LEN = 256
MEM_WIDTH = D_MODEL // 4
MEM_HEADS = 4
MEM_HEAD_DIM = MEM_WIDTH // MEM_HEADS
MIX_WIDTH = RWKV_WIDTH + NSA_WIDTH + MEM_WIDTH
ROPE_THETA = 500000.0
ROPE_DIM = HEAD_DIM // 4
Q_BLOCK = 128
NORM_EPS = 1e-6
NEG_INF = -1e30
FORCE_SCORE = 1e4

RWKV_SIZES = (RWKV_WIDTH, RWKV_WIDTH, RWKV_WIDTH, RWKV_WIDTH, DECAY_LORA, ICLR_LORA)
NSA_SIZES = (NSA_WIDTH, NSA_WIDTH, NSA_HEADS * N_BRANCH) + (HEAD_DIM,) * 6
MEM_SIZES = (MEM_WIDTH, MEM_WIDTH)
RWKV_COLS = sum(RWKV_SIZES)
NSA_COLS = sum(NSA_SIZES)
MEM_COLS = sum(MEM_SIZES)
IN_COLS = RWKV_COLS + NSA_COLS + MEM_COLS


def split_cols(p, sizes):
    offs = [int(o) for o in np.cumsum(sizes)[:-1]]
    return jnp.split(p, offs, axis=-1)

def rms_norm(x, g, eps=NORM_EPS):
    xf = x.astype(jnp.float32)
    y = xf * lax.rsqrt(jnp.mean(xf * xf, axis=-1, keepdims=True) + eps)
    return (y * g.astype(jnp.float32)).astype(x.dtype)

def partial_rope(x, pos):
    half = ROPE_DIM // 2
    inv_freq = ROPE_THETA ** (-jnp.arange(half, dtype=jnp.float32) / half)
    ang = pos.astype(jnp.float32)[:, None] * inv_freq[None, :]
    cos = jnp.cos(ang)[:, None, :]
    sin = jnp.sin(ang)[:, None, :]
    xf = x.astype(jnp.float32)
    x1 = xf[..., :half]
    x2 = xf[..., half:ROPE_DIM]
    out = jnp.concatenate([x1 * cos - x2 * sin, x2 * cos + x1 * sin, xf[..., ROPE_DIM:]], axis=-1)
    return out.astype(x.dtype)

def masked_softmax(s, mask):
    s = jnp.where(mask, s.astype(jnp.float32), NEG_INF)
    m = jnp.max(s, axis=-1, keepdims=True)
    e = jnp.exp(s - m) * mask
    return e / jnp.maximum(jnp.sum(e, axis=-1, keepdims=True), 1e-30)

def head_rms_norm(o, g):
    of = o.astype(jnp.float32)
    y = of * lax.rsqrt(jnp.mean(of * of, axis=-1, keepdims=True) + NORM_EPS)
    return (y * g.astype(jnp.float32)).astype(o.dtype)

def rwkv7_scan(r, decay, k, v, kk, a):
    B, T, H, N = r.shape

    def step(S, inp):
        r_t, w_t, k_t, v_t, kk_t, a_t = inp
        sa = jnp.einsum('bhvk,bhk->bhv', S, -kk_t)
        S = (S * w_t[:, :, None, :]
             + sa[..., None] * (kk_t * a_t)[:, :, None, :]
             + v_t[..., None] * k_t[:, :, None, :])
        y = jnp.einsum('bhvk,bhk->bhv', S, r_t)
        return S, y

    xs = tuple(jnp.moveaxis(u, 1, 0) for u in (r, decay, k, v, kk, a))
    S0 = jnp.zeros((B, H, N, N), jnp.float32)
    _, y = lax.scan(step, S0, xs)
    return jnp.moveaxis(y, 0, 1)

def rwkv7_group(p, mu, w0, w_up, a0, a_up, k_k, k_a, r_k, ln_w, ln_b):
    B, T, _ = p.shape
    H, N = RWKV_HEADS, HEAD_DIM
    pf = p.astype(jnp.float32)
    prev = jnp.pad(pf, ((0, 0), (1, 0), (0, 0)))[:, :-1]
    pf = pf + mu * (prev - pf)
    r, k, v, gate, wd, ad = split_cols(pf, RWKV_SIZES)
    w_log = -jax.nn.softplus(-(w0 + jnp.tanh(wd) @ w_up)) - 0.5
    decay = jnp.exp(-jnp.exp(w_log))
    a = jax.nn.sigmoid(a0 + ad @ a_up)
    kk = k * k_k
    k = k * (1.0 + (a - 1.0) * k_a)
    r, k, v, kk, a, decay = (u.reshape(B, T, H, N) for u in (r, k, v, kk, a, decay))
    kk = kk / jnp.maximum(jnp.sqrt(jnp.sum(kk * kk, axis=-1, keepdims=True)), 1e-12)
    y = rwkv7_scan(r, decay, k, v, kk, a)
    mean = jnp.mean(y, axis=-1, keepdims=True)
    var = jnp.mean(jnp.square(y - mean), axis=-1, keepdims=True)
    y = (y - mean) * lax.rsqrt(var + RWKV_GN_EPS) * ln_w.reshape(H, N) + ln_b.reshape(H, N)
    y = y + jnp.sum(r * k * r_k, axis=-1, keepdims=True) * v
    y = y.reshape(B, T, RWKV_WIDTH) * jax.nn.silu(gate)
    return y.astype(p.dtype)

def nsa_group(p, pos, cmp_pos, ck_w1, ck_w2, cv_w1, cv_w2, gate_b, out_g):
    B, T, _ = p.shape
    Hn, D = NSA_HEADS, HEAD_DIM
    q, gate, glog, kc, vc, ks, vs, kw, vw = split_cols(p, NSA_SIZES)
    q = q.reshape(B, T, Hn, D)
    q_rope = partial_rope(q, pos)
    ks = partial_rope(ks[:, :, None, :], pos)[:, :, 0]
    kw = partial_rope(kw[:, :, None, :], pos)[:, :, 0]
    scale = HEAD_DIM ** -0.5

    n_cmp = (T - CMP_BLOCK) // CMP_STRIDE + 1
    blk = jnp.arange(n_cmp)[:, None] * CMP_STRIDE + jnp.arange(CMP_BLOCK)[None, :]

    def compress(u, w1, w2):
        ub = (u[:, blk] + cmp_pos).reshape(B, n_cmp, CMP_BLOCK * D)
        return jax.nn.silu(ub @ w1) @ w2

    k_cmp = compress(kc, ck_w1, ck_w2)
    v_cmp = compress(vc, cv_w1, cv_w2)
    cmp_end = blk[:, -1]

    n_sel = T // SEL_BLOCK
    n_top = min(SEL_TOPK, n_sel)
    sel_start = jnp.arange(n_sel) * SEL_BLOCK
    overlap = jnp.clip(jnp.minimum(blk[:, -1:] + 1, sel_start[None, :] + SEL_BLOCK)
                       - jnp.maximum(blk[:, :1], sel_start[None, :]), 0, None)
    overlap = overlap.astype(jnp.float32) / CMP_BLOCK
    k_sel_blk = ks.reshape(B, n_sel, SEL_BLOCK, D)
    v_sel_blk = vs.reshape(B, n_sel, SEL_BLOCK, D)
    blk_id = jnp.arange(n_sel)

    kw_pad = jnp.pad(kw, ((0, 0), (WINDOW, 0), (0, 0)))
    vw_pad = jnp.pad(vw, ((0, 0), (WINDOW, 0), (0, 0)))

    def per_block(qb):
        t0 = qb * Q_BLOCK
        tq = t0 + jnp.arange(Q_BLOCK)
        qn = lax.dynamic_slice_in_dim(q, t0, Q_BLOCK, axis=1)
        qr = lax.dynamic_slice_in_dim(q_rope, t0, Q_BLOCK, axis=1)
        s_c = jnp.einsum('bqhd,bcd->bhqc', qn, k_cmp) * scale
        p_c = masked_softmax(s_c, cmp_end[None, :] <= tq[:, None])
        o_c = jnp.einsum('bhqc,bcd->bqhd', p_c.astype(v_cmp.dtype), v_cmp)
        imp = jnp.einsum('bhqc,cs->bqs', p_c, overlap)
        cur = tq // SEL_BLOCK
        valid = blk_id[None, :] <= cur[:, None]
        forced = (blk_id[None, :] == 0) | (blk_id[None, :] == cur[:, None]) | (blk_id[None, :] == cur[:, None] - 1)
        score = jnp.where(forced, FORCE_SCORE, jnp.where(valid, imp, -1.0))
        _, idx = lax.top_k(score, n_top)
        kg = jax.vmap(lambda kb, ib: kb[ib])(k_sel_blk, idx).reshape(B, Q_BLOCK, n_top * SEL_BLOCK, D)
        vg = jax.vmap(lambda vb, ib: vb[ib])(v_sel_blk, idx).reshape(B, Q_BLOCK, n_top * SEL_BLOCK, D)
        kpos = (idx[..., None] * SEL_BLOCK + jnp.arange(SEL_BLOCK)).reshape(B, Q_BLOCK, n_top * SEL_BLOCK)
        s_s = jnp.einsum('bqhd,bqkd->bhqk', qr, kg) * scale
        p_s = masked_softmax(s_s, (kpos <= tq[None, :, None])[:, None])
        o_s = jnp.einsum('bhqk,bqkd->bqhd', p_s.astype(vg.dtype), vg)
        kwb = lax.dynamic_slice_in_dim(kw_pad, t0, Q_BLOCK + WINDOW, axis=1)
        vwb = lax.dynamic_slice_in_dim(vw_pad, t0, Q_BLOCK + WINDOW, axis=1)
        wpos = t0 - WINDOW + jnp.arange(Q_BLOCK + WINDOW)
        diff = tq[:, None] - wpos[None, :]
        m_w = (diff >= 0) & (diff < WINDOW) & (wpos[None, :] >= 0)
        s_w = jnp.einsum('bqhd,bkd->bhqk', qr, kwb) * scale
        p_w = masked_softmax(s_w, m_w)
        o_w = jnp.einsum('bhqk,bkd->bqhd', p_w.astype(vwb.dtype), vwb)
        return o_c, o_s, o_w

    o_c, o_s, o_w = lax.map(per_block, jnp.arange(T // Q_BLOCK))
    o_c, o_s, o_w = (jnp.moveaxis(o, 0, 1).reshape(B, T, Hn, D) for o in (o_c, o_s, o_w))
    g = jax.nn.sigmoid(glog.reshape(B, T, Hn, N_BRANCH) + gate_b.reshape(Hn, N_BRANCH))
    o = g[..., 0:1] * o_c + g[..., 1:2] * o_s + g[..., 2:3] * o_w
    o = head_rms_norm(o, out_g.reshape(Hn, D))
    return o.reshape(B, T, NSA_WIDTH) * jax.nn.silu(gate)

def memory_group(p, mem_k, mem_v, out_g):
    B, T, _ = p.shape
    q, gate = split_cols(p, MEM_SIZES)
    q = q.reshape(B, T, MEM_HEADS, MEM_HEAD_DIM)
    s = jnp.einsum('bthd,bmhd->bhtm', q, mem_k) * (MEM_HEAD_DIM ** -0.5)
    prob = jax.nn.softmax(s.astype(jnp.float32), axis=-1)
    o = jnp.einsum('bhtm,bmhd->bthd', prob.astype(mem_v.dtype), mem_v)
    o = head_rms_norm(o, out_g.reshape(MEM_HEADS, MEM_HEAD_DIM))
    return o.reshape(B, T, MEM_WIDTH) * jax.nn.silu(gate)

def first_inputs(seed: int = 0) -> dict:
    key = jax.random.key(seed)
    ks = jax.random.split(key, 32)
    L = DEPTH
    f32 = jnp.float32

    def nrm(k, shape, scale):
        return jax.random.normal(k, shape, f32) * scale

    def gain(k, shape):
        return 1.0 + 0.05 * jax.random.normal(k, shape, f32)

    cmp_in = CMP_BLOCK * HEAD_DIM
    return {
        'x': nrm(ks[0], (BATCH, SEQ, D_MODEL), 1.0),
        'mem': nrm(ks[1], (BATCH, MEM_LEN, D_MODEL), 1.0),
        'norm_in_g': gain(ks[2], (L, D_MODEL)),
        'w_in': nrm(ks[3], (L, D_MODEL, IN_COLS), D_MODEL ** -0.5),
        'rwkv_mu': jax.random.uniform(ks[4], (L, RWKV_COLS), f32, 0.2, 0.8),
        'rwkv_w0': jax.random.uniform(ks[5], (L, RWKV_WIDTH), f32, -5.0, -1.0),
        'rwkv_w_up': nrm(ks[6], (L, DECAY_LORA, RWKV_WIDTH), 0.1 * DECAY_LORA ** -0.5),
        'rwkv_a0': nrm(ks[7], (L, RWKV_WIDTH), 0.5),
        'rwkv_a_up': nrm(ks[8], (L, ICLR_LORA, RWKV_WIDTH), ICLR_LORA ** -0.5),
        'rwkv_k_k': 0.85 + 0.05 * jax.random.normal(ks[9], (L, RWKV_WIDTH), f32),
        'rwkv_k_a': 1.0 + 0.05 * jax.random.normal(ks[10], (L, RWKV_WIDTH), f32),
        'rwkv_r_k': nrm(ks[11], (L, RWKV_HEADS, HEAD_DIM), 0.1),
        'rwkv_ln_w': gain(ks[12], (L, RWKV_WIDTH)),
        'rwkv_ln_b': nrm(ks[13], (L, RWKV_WIDTH), 0.02),
        'nsa_cmp_pos': nrm(ks[14], (L, CMP_BLOCK, HEAD_DIM), 0.1),
        'nsa_cmp_k_w1': nrm(ks[15], (L, cmp_in, HEAD_DIM), cmp_in ** -0.5),
        'nsa_cmp_k_w2': nrm(ks[16], (L, HEAD_DIM, HEAD_DIM), HEAD_DIM ** -0.5),
        'nsa_cmp_v_w1': nrm(ks[17], (L, cmp_in, HEAD_DIM), cmp_in ** -0.5),
        'nsa_cmp_v_w2': nrm(ks[18], (L, HEAD_DIM, HEAD_DIM), HEAD_DIM ** -0.5),
        'nsa_gate_b': nrm(ks[19], (L, NSA_HEADS * N_BRANCH), 0.1),
        'nsa_out_g': gain(ks[20], (L, NSA_WIDTH)),
        'mem_norm_g': gain(ks[21], (L, D_MODEL)),
        'w_mem_kv': nrm(ks[22], (L, D_MODEL, 2 * MEM_WIDTH), D_MODEL ** -0.5),
        'mem_out_g': gain(ks[23], (L, MEM_WIDTH)),
        'w_out': nrm(ks[24], (L, MIX_WIDTH, D_MODEL), MIX_WIDTH ** -0.5),
        'norm_final_g': gain(ks[25], (D_MODEL,)),
    }

def first_block(x, mem, norm_in_g, w_in, rwkv_mu, rwkv_w0, rwkv_w_up, rwkv_a0, rwkv_a_up,
              rwkv_k_k, rwkv_k_a, rwkv_r_k, rwkv_ln_w, rwkv_ln_b, nsa_cmp_pos, nsa_cmp_k_w1,
              nsa_cmp_k_w2, nsa_cmp_v_w1, nsa_cmp_v_w2, nsa_gate_b, nsa_out_g, mem_norm_g,
              w_mem_kv, mem_out_g, w_out, norm_final_g):
    B, T, _ = x.shape
    M = mem.shape[1]
    pos = jnp.arange(T)
    for l in range(DEPTH):
        h = rms_norm(x, norm_in_g[l])
        p = h @ w_in[l]
        p_rwkv, p_nsa, p_mem = jnp.split(p, [RWKV_COLS, RWKV_COLS + NSA_COLS], axis=-1)
        y_rwkv = rwkv7_group(p_rwkv, rwkv_mu[l], rwkv_w0[l], rwkv_w_up[l], rwkv_a0[l], rwkv_a_up[l],
                             rwkv_k_k[l], rwkv_k_a[l], rwkv_r_k[l], rwkv_ln_w[l], rwkv_ln_b[l])
        y_nsa = nsa_group(p_nsa, pos, nsa_cmp_pos[l], nsa_cmp_k_w1[l], nsa_cmp_k_w2[l],
                          nsa_cmp_v_w1[l], nsa_cmp_v_w2[l], nsa_gate_b[l], nsa_out_g[l])
        kv = rms_norm(mem, mem_norm_g[l]) @ w_mem_kv[l]
        mem_k, mem_v = jnp.split(kv.reshape(B, M, 2, MEM_HEADS, MEM_HEAD_DIM), 2, axis=2)
        y_mem = memory_group(p_mem, mem_k[:, :, 0], mem_v[:, :, 0], mem_out_g[l])
        y = jnp.concatenate([y_rwkv.astype(x.dtype), y_nsa.astype(x.dtype), y_mem.astype(x.dtype)], axis=-1)
        x = x + y @ w_out[l]
    return rms_norm(x, norm_final_g)


DEPTH_2 = 2

CHUNK = 64
QBLOCK = 128
EPS = 1e-6

DIFF_HEADS = 4
DIFF_DK = 64
DIFF_DV = 2 * DIFF_DK
DIFF_SCALE = DIFF_DK ** -0.5
MLA_HEADS = 4
MLA_NOPE = 128
MLA_ROPE = 64
MLA_DV = 128
MLA_Q_LORA = 256
MLA_KV_LORA = 128
MLA_SCALE = (MLA_NOPE + MLA_ROPE) ** -0.5
ROPE_BASE = 10000.0
EVEN_SPLITS = (DIFF_HEADS * 2 * DIFF_DK, DIFF_HEADS * 2 * DIFF_DK, DIFF_HEADS * DIFF_DV, MLA_Q_LORA, MLA_KV_LORA, MLA_ROPE)
EVEN_IN = sum(EVEN_SPLITS)
EVEN_MIX = DIFF_HEADS * DIFF_DV + MLA_HEADS * MLA_DV
SB_HEADS = 16
SB_DH = 64
SB_WIDTH = SB_HEADS * SB_DH
SB_SCALE = SB_DH ** -0.5
XA_HEADS = 4
XA_DH = D_MODEL // XA_HEADS
D_FF = 4 * D_MODEL

N_EVEN = (DEPTH_2 + 1) // 2
N_ODD = DEPTH_2 // 2


def _rms(x, g):
    xf = x.astype(jnp.float32)
    y = xf * lax.rsqrt(jnp.mean(xf * xf, axis=-1, keepdims=True) + EPS)
    return (y * g.astype(jnp.float32)).astype(x.dtype)

def _heads(x, h):
    b, s, _ = x.shape
    return x.reshape(b, s, h, -1).transpose(0, 2, 1, 3)

def _merge(x):
    b, h, s, d = x.shape
    return x.transpose(0, 2, 1, 3).reshape(b, s, h * d)

def _rope(x, pos):
    half = x.shape[-1] // 2
    inv = ROPE_BASE ** (-jnp.arange(half, dtype=jnp.float32) / half)
    ang = pos.astype(jnp.float32)[:, None] * inv[None, :]
    cos, sin = jnp.cos(ang), jnp.sin(ang)
    xf = x.astype(jnp.float32)
    x1, x2 = xf[..., :half], xf[..., half:]
    return jnp.concatenate([x1 * cos - x2 * sin, x2 * cos + x1 * sin], axis=-1).astype(x.dtype)

def _chunk_mask(t, s):
    return (s // CHUNK)[None, :] <= (t // CHUNK)[:, None]

def _sweep(block_fn, qs):
    b, _, s, _ = qs[0].shape
    nb = s // QBLOCK
    qs_b = tuple(jnp.moveaxis(q.reshape(b, q.shape[1], nb, QBLOCK, q.shape[-1]), 2, 0) for q in qs)
    out = lax.map(lambda a: block_fn(a[0], *a[1]), (jnp.arange(nb), qs_b))
    out = jnp.moveaxis(out, 0, 2)
    return out.reshape(b, out.shape[1], s, out.shape[-1])

def _even_mixer(h, w_in, lq1, lk1, lq2, lk2, g_sub, g_cq, w_uq, g_ckv, w_ukv, w_out, lambda_init):
    b, s, _ = h.shape
    pos = jnp.arange(s)
    proj = h @ w_in
    cuts = np.cumsum(EVEN_SPLITS)[:-1].tolist()
    aq, ak, av, cq, ckv, kr = jnp.split(proj, cuts, axis=-1)

    aq = aq.reshape(b, s, DIFF_HEADS, 2, DIFF_DK)
    ak = ak.reshape(b, s, DIFF_HEADS, 2, DIFF_DK)
    q1 = aq[:, :, :, 0].transpose(0, 2, 1, 3)
    q2 = aq[:, :, :, 1].transpose(0, 2, 1, 3)
    k1 = ak[:, :, :, 0].transpose(0, 2, 1, 3)
    k2 = ak[:, :, :, 1].transpose(0, 2, 1, 3)
    va = _heads(av, DIFF_HEADS)
    lam = (jnp.exp(jnp.sum(lq1.astype(jnp.float32) * lk1.astype(jnp.float32)))
           - jnp.exp(jnp.sum(lq2.astype(jnp.float32) * lk2.astype(jnp.float32))) + lambda_init)
    slopes = 2.0 ** (-8.0 * jnp.arange(1, DIFF_HEADS + 1, dtype=jnp.float32) / DIFF_HEADS)

    def diff_block(i, q1b, q2b):
        t = i * QBLOCK + jnp.arange(QBLOCK)
        mask = _chunk_mask(t, pos)
        dist = jnp.abs(t[:, None] - pos[None, :]).astype(jnp.float32)
        bias = -slopes[:, None, None] * dist[None]

        def probs(qb, kk):
            sc = jnp.einsum('bhqd,bhkd->bhqk', qb, kk).astype(jnp.float32) * DIFF_SCALE + bias
            return jax.nn.softmax(jnp.where(mask, sc, -jnp.inf), axis=-1)

        p = probs(q1b, k1) - lam * probs(q2b, k2)
        return jnp.einsum('bhqk,bhkd->bhqd', p.astype(va.dtype), va)

    o_a = _sweep(diff_block, (q1, q2))
    o_a = _rms(o_a, g_sub) * (1.0 - lambda_init)

    q = _heads(_rms(cq, g_cq) @ w_uq, MLA_HEADS)
    q_nope, q_rope = q[..., :MLA_NOPE], _rope(q[..., MLA_NOPE:], pos)
    kv = _heads(_rms(ckv, g_ckv) @ w_ukv, MLA_HEADS)
    k_nope, vb = kv[..., :MLA_NOPE], kv[..., MLA_NOPE:]
    k_rope = _rope(kr, pos)

    def mla_block(i, qnb, qrb):
        t = i * QBLOCK + jnp.arange(QBLOCK)
        mask = _chunk_mask(t, pos)
        sc = (jnp.einsum('bhqd,bhkd->bhqk', qnb, k_nope)
              + jnp.einsum('bhqr,bkr->bhqk', qrb, k_rope)).astype(jnp.float32) * MLA_SCALE
        p = jax.nn.softmax(jnp.where(mask, sc, -jnp.inf), axis=-1)
        return jnp.einsum('bhqk,bhkd->bhqd', p.astype(vb.dtype), vb)

    o_b = _sweep(mla_block, (q_nope, q_rope))

    return jnp.concatenate([_merge(o_a), _merge(o_b)], axis=-1) @ w_out

def _odd_mixer(h, w_in, w_out):
    s = h.shape[1]
    pos = jnp.arange(s)
    q, k, v = jnp.split(h @ w_in, 3, axis=-1)
    q, k, v = _heads(q, SB_HEADS), _heads(k, SB_HEADS), _heads(v, SB_HEADS)

    def sb_block(i, qb):
        t = i * QBLOCK + jnp.arange(QBLOCK)
        strict = pos[None, :] < t[:, None]
        z = jnp.einsum('bhqd,bhkd->bhqk', qb, k).astype(jnp.float32) * SB_SCALE
        log_beta = jax.nn.log_sigmoid(z)
        log_keep = jnp.where(strict, jax.nn.log_sigmoid(-z), 0.0)
        between = lax.cumsum(log_keep, axis=3, reverse=True) - log_keep
        a = jnp.where(strict, jnp.exp(log_beta + between), 0.0)
        return jnp.einsum('bhqk,bhkd->bhqd', a.astype(v.dtype), v)

    o = _sweep(sb_block, (q,))
    return _merge(o) @ w_out

def _cross(h, mem_n, wq, wkv, wo):
    q = _heads(h @ wq, XA_HEADS)
    k, v = jnp.split(mem_n @ wkv, 2, axis=-1)
    k, v = _heads(k, XA_HEADS), _heads(v, XA_HEADS)
    sc = jnp.einsum('bhqd,bhkd->bhqk', q, k).astype(jnp.float32) * (XA_DH ** -0.5)
    p = jax.nn.softmax(sc, axis=-1)
    return _merge(jnp.einsum('bhqk,bhkd->bhqd', p.astype(v.dtype), v)) @ wo

def _mlp(h, w1, w2):
    return jnp.square(jax.nn.relu(h @ w1)) @ w2

def second_inputs(seed: int = 0) -> dict:
    key = jax.random.key(seed)
    ks = iter(jax.random.split(key, 40))

    def nrm(shape, scale):
        return jax.random.normal(next(ks), shape, jnp.float32) * scale

    def gain(shape):
        return 1.0 + nrm(shape, 0.02)

    L, E, O, D = DEPTH_2, N_EVEN, N_ODD, D_MODEL
    return {
        'x': nrm((BATCH, SEQ, D), 1.0),
        'mem': nrm((BATCH, MEM_LEN, D), 1.0),
        'ev_norm': gain((E, D)),
        'ev_w_in': nrm((E, D, EVEN_IN), D ** -0.5),
        'diff_lq1': nrm((E, DIFF_DK), 0.1),
        'diff_lk1': nrm((E, DIFF_DK), 0.1),
        'diff_lq2': nrm((E, DIFF_DK), 0.1),
        'diff_lk2': nrm((E, DIFF_DK), 0.1),
        'diff_subln': gain((E, DIFF_DV)),
        'mla_g_cq': gain((E, MLA_Q_LORA)),
        'mla_w_uq': nrm((E, MLA_Q_LORA, MLA_HEADS * (MLA_NOPE + MLA_ROPE)), MLA_Q_LORA ** -0.5),
        'mla_g_ckv': gain((E, MLA_KV_LORA)),
        'mla_w_ukv': nrm((E, MLA_KV_LORA, MLA_HEADS * (MLA_NOPE + MLA_DV)), MLA_KV_LORA ** -0.5),
        'ev_w_out': nrm((E, EVEN_MIX, D), EVEN_MIX ** -0.5),
        'od_norm': gain((O, D)),
        'sb_w_in': nrm((O, D, 3 * SB_WIDTH), D ** -0.5),
        'sb_w_out': nrm((O, SB_WIDTH, D), SB_WIDTH ** -0.5),
        'xa_norm': gain((L, D)),
        'xa_mem_norm': gain((L, D)),
        'xa_wq': nrm((L, D, D), D ** -0.5),
        'xa_wkv': nrm((L, D, 2 * D), D ** -0.5),
        'xa_wo': nrm((L, D, D), D ** -0.5),
        'mlp_norm': gain((L, D)),
        'mlp_w1': nrm((L, D, D_FF), D ** -0.5),
        'mlp_w2': nrm((L, D_FF, D), D_FF ** -0.5),
        'final_norm': gain((D,)),
    }

def second_block(x, mem, ev_norm, ev_w_in, diff_lq1, diff_lk1, diff_lq2, diff_lk2, diff_subln,
              mla_g_cq, mla_w_uq, mla_g_ckv, mla_w_ukv, ev_w_out, od_norm, sb_w_in, sb_w_out,
              xa_norm, xa_mem_norm, xa_wq, xa_wkv, xa_wo, mlp_norm, mlp_w1, mlp_w2, final_norm):
    h = x
    for i in range(DEPTH_2):
        j = i // 2
        if i % 2 == 0:
            lambda_init = 0.8 - 0.6 * math.exp(-0.3 * i)
            h = h + _even_mixer(_rms(h, ev_norm[j]), ev_w_in[j], diff_lq1[j], diff_lk1[j], diff_lq2[j],
                                diff_lk2[j], diff_subln[j], mla_g_cq[j], mla_w_uq[j], mla_g_ckv[j],
                                mla_w_ukv[j], ev_w_out[j], lambda_init)
        else:
            h = h + _odd_mixer(_rms(h, od_norm[j]), sb_w_in[j], sb_w_out[j])
        h = h + _cross(_rms(h, xa_norm[i]), _rms(mem, xa_mem_norm[i]), xa_wq[i], xa_wkv[i], xa_wo[i])
        h = h + _mlp(_rms(h, mlp_norm[i]), mlp_w1[i], mlp_w2[i])
    return _rms(h, final_norm)


def setup_inputs(seed=0):
    out = dict(first_inputs(seed))
    for name, value in second_inputs(seed + 1).items():
        if name != "x":
            out[name + "_2"] = value
    return out


def reference(
    x, mem, norm_in_g, w_in, rwkv_mu, rwkv_w0, rwkv_w_up, rwkv_a0, rwkv_a_up, rwkv_k_k,
    rwkv_k_a, rwkv_r_k, rwkv_ln_w, rwkv_ln_b, nsa_cmp_pos, nsa_cmp_k_w1, nsa_cmp_k_w2,
    nsa_cmp_v_w1, nsa_cmp_v_w2, nsa_gate_b, nsa_out_g, mem_norm_g, w_mem_kv, mem_out_g, w_out,
    norm_final_g, mem_2, ev_norm_2, ev_w_in_2, diff_lq1_2, diff_lk1_2, diff_lq2_2, diff_lk2_2,
    diff_subln_2, mla_g_cq_2, mla_w_uq_2, mla_g_ckv_2, mla_w_ukv_2, ev_w_out_2, od_norm_2,
    sb_w_in_2, sb_w_out_2, xa_norm_2, xa_mem_norm_2, xa_wq_2, xa_wkv_2, xa_wo_2, mlp_norm_2,
    mlp_w1_2, mlp_w2_2, final_norm_2,
):
    x = first_block(
        x, mem, norm_in_g, w_in, rwkv_mu, rwkv_w0, rwkv_w_up, rwkv_a0, rwkv_a_up, rwkv_k_k,
        rwkv_k_a, rwkv_r_k, rwkv_ln_w, rwkv_ln_b, nsa_cmp_pos, nsa_cmp_k_w1, nsa_cmp_k_w2,
        nsa_cmp_v_w1, nsa_cmp_v_w2, nsa_gate_b, nsa_out_g, mem_norm_g, w_mem_kv, mem_out_g,
        w_out, norm_final_g,
    )
    return second_block(
        x, mem_2, ev_norm_2, ev_w_in_2, diff_lq1_2, diff_lk1_2, diff_lq2_2, diff_lk2_2,
        diff_subln_2, mla_g_cq_2, mla_w_uq_2, mla_g_ckv_2, mla_w_ukv_2, ev_w_out_2, od_norm_2,
        sb_w_in_2, sb_w_out_2, xa_norm_2, xa_mem_norm_2, xa_wq_2, xa_wkv_2, xa_wo_2, mlp_norm_2,
        mlp_w1_2, mlp_w2_2, final_norm_2,
    )


_drawn_inputs = setup_inputs


def setup_inputs(seed=0):
    import zlib

    import numpy as np

    out = dict(_drawn_inputs(seed))
    spreads = {}
    factors = {'rwkv_w_up': 8.0,
     'rwkv_k_k': 3.803,
     'rwkv_ln_w': 3.191,
     'rwkv_ln_b': 6.769,
     'nsa_gate_b': 4.463,
     'nsa_out_g': 2.962,
     'mem_out_g': 2.835,
     'ev_norm_2': 3.02,
     'diff_lq1_2': 8.0,
     'diff_subln_2': 5.265,
     'mla_g_cq_2': 8.0,
     'mla_g_ckv_2': 8.0,
     'od_norm_2': 6.231,
     'xa_norm_2': 8.0,
     'xa_mem_norm_2': 8.0,
     'final_norm_2': 2.845}
    for name, (base, spread) in spreads.items():
        noise = np.random.default_rng([zlib.crc32(name.encode()), seed]).standard_normal(out[name].shape)
        drawn = base * np.exp(spread * noise) if base else spread * noise
        out[name] = jnp.asarray(drawn.astype(out[name].dtype))
    for name, factor in factors.items():
        out[name] = (out[name] * factor).astype(out[name].dtype)
    return out
```

```python
from contextlib import ExitStack

import concourse.bass as bass
from concourse import mybir

F32 = mybir.dt.float32
F32R = mybir.dt.float32r
ALU = mybir.AluOpType
ACT = mybir.ActivationFunctionType
AX = mybir.AxisListType.X

P = 128
T = 512
ND = 8
DECAY_C = 0.6065306597126334
NEG = -1e30

UNITS = {
    "w_in": 30, "w_mem_kv": 4, "w_out": 8, "ev_w_in": 16, "ev_w_out": 8, "sb_w_in": 24, "sb_w_out": 8,
    "wq0": 8, "wkv0": 16, "wo0": 8, "w10": 32, "w20": 32,
    "wq1": 8, "wkv1": 16, "wo1": 8, "w11": 32, "w21": 32,
    "uq": 2, "ukv": 1,
}

PCOLS = [
    ("norm_in_g", 8), ("mu", 17), ("w0", 4), ("a0h", 4), ("k_k", 4), ("k_a", 4), ("r_k", 4), ("ln_w", 4), ("ln_b", 4),
    ("nsa_out_g", 2), ("mem_norm_g", 8), ("mem_out_g", 2), ("norm_final_g", 8), ("pos", 32), ("ev_norm", 8),
    ("subln", 1), ("g_cq", 2), ("g_ckv", 1), ("od_norm", 8), ("xa_norm0", 8), ("xa_norm1", 8), ("xa_mem0", 8),
    ("xa_mem1", 8), ("mlp_norm0", 8), ("mlp_norm1", 8), ("final_norm", 8), ("lqk", 4), ("gate_b", 12), ("eps6", 1),
    ("gneps", 1), ("one", 1), ("half", 1),
]
CCOLS = [("ident", 128), ("ones", 128), ("blk", 128), ("ntri", 128), ("nones", 128), ("causal", 128),
         ("rot_n", 128), ("rot_m", 128), ("sbm", 128)]


def offsets(cols):
    at, out = 0, {}
    for name, n in cols:
        out[name] = (at, n)
        at += n
    return out, at


POFF, PN = offsets(PCOLS)
COFF, CN = offsets(CCOLS)


class Engine:

    def __init__(self, eng, sem, link):
        self.eng, self.sem, self.link = eng, sem, link
        self.count, self.seen = 0, {}

    def wait(self, *toks):
        need = {}

        def walk(t):
            if t is None:
                return
            if isinstance(t, list):
                for x in t:
                    walk(x)
                return
            if t[0] is self.sem and not self.link:
                return
            need[id(t[0])] = (t[0], max(t[1], need.get(id(t[0]), (None, 0))[1]))

        walk(list(toks))
        for key, (sem, value) in need.items():
            if self.seen.get(key, 0) < value:
                self.seen[key] = value
                if self.eng is not None:
                    self.eng.wait_ge(sem, value)

    def op(self, fn, *toks):
        if self.link and self.count:
            self.wait((self.sem, self.count))
        self.wait(*toks)
        self.count += 1
        if self.eng is not None:
            fn(self.eng).then_inc(self.sem, 1)
        return (self.sem, self.count)

    def many(self, fns, *toks):
        self.wait(*toks)
        self.count += 1
        if self.eng is not None:
            for fn in fns[:-1]:
                fn(self.eng)
            fns[-1](self.eng).then_inc(self.sem, 1)
        return (self.sem, self.count)


class Buf:
    def __init__(self, ap):
        self.ap, self.free = ap, []

    def __getitem__(self, key):
        return self.ap[key]


class Pool:

    def __init__(self, aps):
        self.items = [Buf(a) for a in aps]
        self.low = len(aps)

    def get(self):
        assert self.items, "no free buffer"
        b = self.items.pop(0)
        self.low = min(self.low, len(self.items))
        return b

    def put(self, b, *toks):
        b.free = list(toks)
        self.items.append(b)


def par(gens, width):
    gens, live = list(gens), []
    while gens or live:
        while gens and len(live) < width:
            live.append(gens.pop(0))
        for g in list(live):
            try:
                next(g)
            except StopIteration:
                live.remove(g)
            yield


def drive(gen):
    for _ in gen:
        pass


def plan(env, order):
    S, V, A, G, PE = env.S, env.V, env.A, env.G, env.PE
    dram, sems = env.dram, env.sems
    psum, pool, ptp = Pool(env.psum), Pool(env.tiles), Pool(env.pt)
    raw, wr = Pool(env.raw), Pool(env.wr)
    ahi, alo = [Buf(a) for a in env.ahi], [Buf(a) for a in env.alo]
    hhi, hlo = [Buf(a) for a in env.hhi], [Buf(a) for a in env.hlo]
    X = [Buf(a) for a in env.x]
    stats = Pool(env.stats)
    cst, pv = env.cst, env.pv

    def C(name):
        o, n = COFF[name]
        return cst[:, o:o + n]

    def PV(name, i=0, n=1):
        o, _ = POFF[name]
        return pv[:, o + i:o + i + n]

    dcount = {}

    def load(dst, src, key, *toks):
        sem = sems[key]
        S.wait(*toks)
        dcount[key] = dcount.get(key, 0) + 16
        if S.eng is not None:
            S.eng.dma_start(dst, src).then_inc(sem, 16)
        return (sem, dcount[key])

    c_ok = [load(cst[:, :], dram["cst"], "cst"), load(pv[:, :], dram["pvec"], "cst")][-1]
    for i in range(ND):
        X[i].tok = load(X[i][:, :], dram["xT"][i], f"x{i}")
    for e in (V, A, PE, G):
        e.wait(c_ok)

    seen, ready = [], {}
    for n, ra in enumerate(raw.items):
        ra.idx = n

    def convert(n):
        name, u = order[n]
        ra, w = raw.get(), wr.get()
        t = load(ra[:, :], dram[name][u], f"raw{ra.idx}", ra.free)
        hi, lo = w.ap[:, 0:1024], w.ap[:, 1024:2048]
        t1 = A.op(lambda e: e.activation(hi, ra[:, :], ACT.Copy), t, w.free)
        t2 = V.op(lambda e: e.tensor_tensor(lo, ra[:, :], hi.bitcast(F32), ALU.subtract), t1)
        raw.put(ra, t1, t2)
        ready[n] = (w, [t1, t2])

    def weight(name, u):
        n = len(seen)
        seen.append((name, u))
        if order is None:
            return wr.items[0], []
        assert order[n] == (name, u)
        for m in range(n, min(n + env.look, len(order))):
            if m not in ready and m not in done_units:
                convert(m)
        done_units.add(n)
        return ready.pop(n)

    done_units = set()

    def drop(w, *toks):
        if order is not None:
            wr.put(w, *toks)

    def whi(w, k, m0=0, m1=128):
        return w.ap[:, k * 128 + m0:k * 128 + m1]

    def wlo(w, k, m0=0, m1=128):
        return w.ap[:, 1024 + k * 128 + m0:1024 + k * 128 + m1]

    def mm(out, lhsT, rhs, start, stop):
        return lambda e: e.matmul(out, lhsT, rhs, start=start, stop=stop, skip_group_check=True)

    def tr(out, in_, n=128):
        return lambda e: e.transpose(out, in_, C("ident")[0:n, 0:n])

    def fm(bank, w, hi, lo, nk, start=True, stop=True, m=(0, 128), n=(0, T), wk=0, row=0):
        fns = []
        mw = m[1] - m[0]
        out = bank[row:row + mw, 0:n[1] - n[0]]
        for k in range(nk):
            a_hi, a_lo = hi[k][:, n[0]:n[1]], lo[k][:, n[0]:n[1]]
            s = start and k == 0
            e_ = stop and k == nk - 1
            fns += [mm(out, whi(w, wk + k, *m), a_hi, s, False), mm(out, whi(w, wk + k, *m), a_lo, False, False),
                    mm(out, wlo(w, wk + k, *m), a_hi, False, e_)]
        return fns

    def tm(out, w, hi, lo, nk, tt, start, m=(0, 128), wk=0):
        fns = []
        for k in range(nk):
            a_hi, a_lo = hi[k][:, tt * 128:tt * 128 + 128], lo[k][:, tt * 128:tt * 128 + 128]
            fns += [mm(out, a_hi, whi(w, wk + k, *m), start and k == 0, False),
                    mm(out, a_hi, wlo(w, wk + k, *m), False, False),
                    mm(out, a_lo, whi(w, wk + k, *m), False, k == nk - 1)]
        return fns

    def split_scaled(src, scale, hi, lo, *toks):
        t1 = A.op(lambda e: e.activation(hi, src, ACT.Copy, scale=scale), *toks)
        t2 = V.op(lambda e: e.scalar_tensor_tensor(out=lo, in0=src, scalar=scale, in1=hi.bitcast(F32),
                                                   op0=ALU.mult, op1=ALU.subtract), t1)
        return t1, t2

    def split_plain(src, hi, lo, *toks):
        t1 = A.op(lambda e: e.activation(hi, src, ACT.Copy), *toks)
        t2 = V.op(lambda e: e.tensor_tensor(lo, src, hi.bitcast(F32), ALU.subtract), t1)
        return t1, t2

    def rsqrt(dst, src, scale, bias, *toks):
        t = A.op(lambda e: e.activation(dst, src, ACT.Ln, bias=bias, scale=scale), *toks)
        t2 = A.op(lambda e: e.activation(dst, dst, ACT.Exp, scale=-0.5))
        return t, t2

    def silu(dst, src, tmp, *toks):
        t1 = A.op(lambda e: e.activation(tmp, src, ACT.Tanh, scale=0.5), *toks)
        t2 = V.op(lambda e: e.tensor_scalar(tmp, tmp, 1.0, 0.5, ALU.add, ALU.mult), t1)
        return V.op(lambda e: e.tensor_tensor(dst, tmp, src, ALU.mult), t2)

    class Norm:
        pass

    def squares(tiles, n, acc):
        tmp = pool.get()
        t = None
        for i, (ap, tok) in enumerate(tiles):
            dst = acc if i == 0 else tmp.ap[:, 0:n]
            ts = A.op(lambda e, dst=dst, ap=ap: e.activation(dst, ap, ACT.Square), tok, t,
                      acc_free if i == 0 else tmp.free)
            if i:
                t = V.op(lambda e: e.tensor_tensor(acc, acc, tmp.ap[:, 0:n], ALU.add), ts)
            else:
                t = ts
        pool.put(tmp, t)
        return t

    acc_free = None

    def stats_of(acc, n, t_acc, d, want_col, eps="eps6"):
        R = pool.get()
        b = psum.get()
        t = PE.many([mm(b[:, 0:n], C("ones"), acc, True, True)], t_acc, b.free)
        t1, tR = rsqrt(R[:, 0:n], b[:, 0:n], 1.0 / d, PV(eps), t, R.free)
        psum.put(b, t1)
        out = Norm()
        out.R, out.tR = R, tR
        if want_col:
            b = psum.get()
            nt = n // 128
            t = PE.many([mm(b[:, j:j + 1], acc[:, j * 128:j * 128 + 128], C("ones")[:, 0:1], True, True)
                         for j in range(nt)], t_acc, b.free)
            col = stats.get()
            t1, tc = rsqrt(col[:, 0:nt], b[:, 0:nt], 1.0 / d, PV(eps), t, col.free)
            psum.put(b, t1)
            out.col, out.tc = col, tc
        out.t_acc_read = t
        return out

    def norm_input(gname, want_col):
        acc = pool.get()
        nonlocal acc_free
        acc_free = acc.free
        for i in range(ND):
            t1, t2 = split_scaled(X[i][:, :], PV(gname, i), ahi[i][:, :], alo[i][:, :], X[i].tok, ahi[i].free,
                                  alo[i].free)
            ahi[i].tok, alo[i].tok = t1, t2
        t = squares([(X[i][:, :], X[i].tok) for i in range(ND)], T, acc.ap)
        nm = stats_of(acc.ap, T, t, 1024, want_col)
        pool.put(acc, nm.t_acc_read)
        nm.act = [[a.tok for a in ahi], [a.tok for a in alo]]
        for i in range(ND):
            X[i].reads = [ahi[i].tok, alo[i].tok, t]
        return nm

    def residual_dense(name, hi, lo, act_toks):
        last = None
        for u in range(ND):
            w, wt = weight(name, u)
            b = psum.get()
            t = PE.many(fm(b, w, hi, lo, ND), wt, act_toks, b.free)
            drop(w, t)
            t2 = V.op(lambda e, u=u, b=b: e.tensor_tensor(X[u][:, :], X[u][:, :], b[:, :], ALU.add), t,
                      X[u].tok, X[u].reads)
            psum.put(b, t2)
            X[u].tok = t2
            last = t
            yield
        for a in hi + lo:
            a.free = [last]

    def attn_head(score, nks, scale, PT, tPT, diag=None, gate=None):
        PT3 = PT.ap.rearrange("p (j q) -> p j q", j=4)
        out = []
        for i in range(4):
            nk = nks[i]
            prods, toks = score(i)
            b = psum.get()
            t = PE.many([mm(b[:, 0:nk], l, r, n == 0, n == len(prods) - 1) for n, (l, r) in enumerate(prods)],
                        toks, b.free)
            if diag is not None:
                dap, td = diag
                t = V.op(lambda e, b=b, nk=nk: e.tensor_tensor(b[:, nk - 128:nk], b[:, nk - 128:nk], dap, ALU.add),
                         t, td)
            st = stats.get()
            t = V.op(lambda e, b=b, st=st, nk=nk: e.tensor_reduce(st[:, 0:1], b[:, 0:nk], AX, ALU.max), t, st.free)
            t = V.op(lambda e, st=st: e.tensor_scalar(st[:, 1:2], st[:, 0:1], -scale, None, ALU.mult))
            pr = pool.get()
            t = A.op(lambda e, b=b, st=st, nk=nk, pr=pr: e.activation(
                pr[:, 0:nk], b[:, 0:nk], ACT.Exp, bias=st[:, 1:2], scale=scale, accum_out=st[:, 2:3]), t, pr.free)
            psum.put(b, t)
            t = V.op(lambda e, st=st: e.reciprocal(st[:, 3:4], st[:, 2:3]), t)
            if gate is not None:
                gap, gt = gate(i)
                t = V.op(lambda e, st=st, gap=gap: e.tensor_tensor(st[:, 3:4], st[:, 3:4], gap, ALU.mult), gt)
            t = V.op(lambda e, st=st, nk=nk, pr=pr: e.tensor_scalar(pr[:, 0:nk], pr[:, 0:nk], st[:, 3:4], None,
                                                                    ALU.mult))
            stats.put(st, t)
            yield
            t = turn(pr, nk, i, PT3, t, tPT)
            pool.put(pr, t[0])
            out.append(t[1])
            yield
        PT.tok = out

    def turn(pr, nk, i, PT3, t, tPT):
        b = psum.get()
        nj = (nk + 127) // 128
        tt = PE.many([tr(b[0:min(128, nk - 128 * j), j * 128:j * 128 + 128], pr[:, j * 128:min(nk, j * 128 + 128)])
                      for j in range(nj)], t, b.free)
        kp = min(nk, 128)
        b3 = b.ap.rearrange("p (j q) -> p j q", j=4)
        t2 = A.op(lambda e: e.activation(PT3[0:kp, 0:nj, i * 128:i * 128 + 128], b3[0:kp, 0:nj, :], ACT.Copy),
                  tt, tPT)
        psum.put(b, t2)
        return tt, t2

    mem_w = [("w_mem_kv", u) for u in range(4)]

    def mem_act(src, gname, m_hi, m_lo):
        tiles = []
        bufs = [pool.get() for _ in range(4)]
        acc = pool.get()
        nonlocal acc_free
        acc_free = acc.free
        for i in range(ND):
            bf = bufs[i // 2]
            ap = bf.ap[:, (i % 2) * 256:(i % 2) * 256 + 256]
            t = load(ap, dram[src][i], "mem", bf.free)
            tiles.append((ap, t))
        for i, (ap, t) in enumerate(tiles):
            t = tiles[-1][1]
            t1, t2 = split_scaled(ap, PV(gname, i), m_hi[i][:, :], m_lo[i][:, :], t, m_hi[i].free, m_lo[i].free)
            m_hi[i].tok, m_lo[i].tok = t1, t2
        t = squares([(ap, tiles[-1][1]) for ap, _ in tiles], 256, acc.ap[:, 0:256])
        nm = stats_of(acc.ap[:, 0:256], 256, t, 1024, True)
        pool.put(acc, nm.t_acc_read)
        for bf in bufs:
            pool.put(bf, t, m_hi[7].tok, m_lo[7].tok)
        nm.act = [[a.tok for a in m_hi], [a.tok for a in m_lo]]
        return nm

    extra = Pool(env.extra)

    def to_pool(keep=()):
        toks = [b.free for b in hhi + hlo]
        kept = [b for b in extra.items if b.pair in keep]
        for b in extra.items:
            if b.pair not in keep:
                b.free = list(toks)
                pool.items.append(b)
        extra.items = kept

    def to_pairs():
        mine = [b for b in pool.items if b.is_extra]
        pool.items = [b for b in pool.items if not b.is_extra]
        toks = [b.free for b in mine] + [b.free for b in hhi + hlo]
        extra.items = extra.items + mine
        assert len(extra.items) == 16
        for b in hhi + hlo:
            b.free = list(toks)

    for b in pool.items:
        b.is_extra = False
    for n, b in enumerate(extra.items):
        b.is_extra, b.pair = True, n % 8

    def mem_pairs():
        m_hi = [Buf(hhi[i // 2].ap[:, (i % 2) * 256:(i % 2) * 256 + 256]) for i in range(ND)]
        m_lo = [Buf(hlo[i // 2].ap[:, (i % 2) * 256:(i % 2) * 256 + 256]) for i in range(ND)]
        for i in range(ND):
            m_hi[i].free, m_lo[i].free = hhi[i // 2].free, hlo[i // 2].free
        return m_hi, m_lo

    def mem_kv(nm, name, nh_tiles, m_hi, m_lo):
        kts = [pool.get() for _ in range(nh_tiles // 2)]
        vts = [pool.get() for _ in range(nh_tiles // 2)]
        n = nh_tiles
        kap = [kts[i // 2].ap[:, (i % 2) * 256:(i % 2) * 256 + 256] for i in range(n)]
        nv = n // 4 if n >= 4 else 1

        def vap(mt, c0, c1):
            if n == 2:
                return vts[0].ap[:, mt * 256 + c0:mt * 256 + c1]
            h = c0 // 512
            return vts[mt * 2 + h].ap[:, c0 - 512 * h:c1 - 512 * h]

        tk, tv = [], []
        t = None
        for u in range(n):
            w, wt = weight(name, u)
            b = psum.get()
            t = PE.many(fm(b, w, m_hi, m_lo, ND, n=(0, 256)), wt, nm.act, b.free)
            drop(w, t)
            t2 = V.op(lambda e, u=u, b=b: e.tensor_tensor(kap[u], b[:, 0:256], nm.R[:, 0:256], ALU.mult), t, nm.tR,
                      kts[u // 2].free)
            psum.put(b, t2)
            tk.append(t2)
            yield
        for u in range(n):
            w, wt = weight(name, n + u)
            b = psum.get()
            fns = []
            for mt in range(2):
                fns += tm(b[:, mt * 128:mt * 128 + 128], w, m_hi, m_lo, ND, mt, mt == 0)
            t = PE.many(fns, wt, nm.act, b.free)
            drop(w, t)
            for mt in range(2):
                t2 = A.op(lambda e, u=u, b=b, mt=mt: e.activation(
                    vap(mt, u * 128, u * 128 + 128), b[:, mt * 128:mt * 128 + 128], ACT.Copy,
                    scale=nm.col[:, mt:mt + 1]), t, nm.tc, [x.free for x in vts])
            psum.put(b, t2)
            tv.append(t2)
            yield
        pool.put(nm.R, tk)
        stats.put(nm.col, tv)
        for b_ in hhi + hlo:
            b_.free = [t]
        nm.kts, nm.vts, nm.kap, nm.vap, nm.tk, nm.tv = kts, vts, kap, vap, tk, tv

    def proj_fm(nm, name, u, dst, dst_free, scale=None, row0=0, m=(0, 128)):
        w, wt = weight(name, u)
        b = psum.get()
        t = PE.many(fm(b, w, ahi, alo, ND, m=m), wt, nm.act, b.free)
        drop(w, t)
        nm.last = t
        mw = m[1] - m[0]
        t2 = V.op(lambda e: e.tensor_tensor(dst, b[0:mw, :], nm.R[0:mw, :], ALU.mult), t, nm.tR, dst_free)
        psum.put(b, t2)
        return t2

    def proj_tm(nm, name, u, dst, dst_free, m=(0, 128), w_=None):
        w, wt = weight(name, u) if w_ is None else w_
        mw = m[1] - m[0]
        b = psum.get()
        fns = []
        for tt in range(4):
            fns += tm(b[:, tt * mw:tt * mw + mw], w, ahi, alo, ND, tt, tt == 0, m=m)
        t = PE.many(fns, wt, nm.act, b.free)
        if w_ is None:
            drop(w, t)
        nm.last = t
        for tt in range(4):
            t2 = A.op(lambda e, tt=tt: e.activation(dst[:, tt, :], b[:, tt * mw:tt * mw + mw], ACT.Copy,
                                                    scale=nm.col[:, tt:tt + 1]), t, nm.tc, dst_free)
        psum.put(b, t2)
        return t2, t

    def r3(ap, n):
        return ap.rearrange("p (j q) -> p j q", j=n)

    def block_norm(y, ty, gcol, dst, extra_mul=None, free=None):
        sq = pool.get()
        t = A.op(lambda e: e.activation(sq[:, :], y, ACT.Square), ty, sq.free)
        b = psum.get()
        t = PE.many([mm(b[:, :], C("blk"), sq[:, :], True, True)], t, b.free)
        t1, t2 = rsqrt(sq[:, :], b[:, :], 1.0 / 64, PV("eps6"), t)
        psum.put(b, t1)
        t = V.op(lambda e: e.scalar_tensor_tensor(out=y, in0=y, scalar=gcol, in1=sq[:, :], op0=ALU.mult,
                                                  op1=ALU.mult), t2)
        pool.put(sq, t)
        return V.op(lambda e: e.tensor_tensor(dst, y, extra_mul, ALU.mult), free)

    Y = [None] * ND

    def rwkv_pair(nm, i, sh):
        def shifted(u, mucol, dst, dfree):
            raw_t = pool.get()
            t = proj_fm(nm, "w_in", u, raw_t[:, :], raw_t.free)
            t1 = V.op(lambda e: e.tensor_scalar(dst, raw_t[:, :], omm[:, mucol:mucol + 1], None, ALU.mult), t,
                      t_omm, dfree)
            t2 = V.op(lambda e: e.scalar_tensor_tensor(
                out=dst[:, 1:T], in0=raw_t[:, 0:T - 1], scalar=PV("mu", mucol), in1=dst[:, 1:T], op0=ALU.mult,
                op1=ALU.add))
            pool.put(raw_t, t2)
            return t2

        g_ = pool.get()
        tg = shifted(13 + i, 12 + i, g_[:, :], g_.free)
        tmp = pool.get()
        tg = silu(g_[:, :], g_[:, :], tmp[:, :], tg, tmp.free)
        yield
        k_ = pool.get()
        tk = shifted(5 + i, 4 + i, k_[:, :], k_.free)
        yield
        b = psum.get()
        t = PE.many([mm(b[:, :], sh.lora[0:64, i * 128:i * 128 + 128], sh.wdad[0:64, :], True, True)], sh.tl, b.free)
        sg = pool.get()
        t1 = A.op(lambda e: e.activation(sg[:, :], b[:, :], ACT.Tanh, bias=w0h[:, i:i + 1], scale=0.5), t, t_omm,
                  sg.free)
        psum.put(b, t1)
        t = V.op(lambda e: e.tensor_scalar(sg[:, :], sg[:, :], 1.0, 0.5, ALU.add, ALU.mult), t1)
        b = psum.get()
        ta = PE.many([mm(b[:, :], sh.lora[64:128, i * 128:i * 128 + 128], sh.wdad[64:128, :], True, True)], sh.tl,
                     b.free)
        a_ = pool.get()
        t1 = A.op(lambda e: e.activation(a_[:, :], b[:, :], ACT.Tanh, bias=a0h[:, i:i + 1], scale=0.5), ta, a_.free)
        psum.put(b, t1)
        ta = V.op(lambda e: e.tensor_scalar(a_[:, :], a_[:, :], 1.0, 0.5, ALU.add, ALU.mult), t1)
        S_, Sx = pool.get(), pool.get()
        s3 = r3(S_.ap, 4)
        for c in range(4):
            cs = slice(c * 128, c * 128 + 128)
            t = V.op(lambda e, cs=cs: e.tensor_tensor_scan(S_[:, cs], C("ones"), sg[:, cs], 0.0, ALU.mult, ALU.add),
                     S_.free, t)
        yield
        st = stats.get()
        t = V.op(lambda e: e.tensor_copy(st[:, 0:4], s3[:, :, 63]), st.free)
        for c in range(4):
            cs = slice(c * 128, c * 128 + 128)
            t = V.op(lambda e, cs=cs, c=c: e.tensor_scalar(S_[:, cs], S_[:, cs], st[:, c:c + 1], None, ALU.subtract))
        t = V.op(lambda e: e.tensor_tensor(st[:, 4:7], s3[:, 0:3, 127], st[:, 1:4], ALU.add))
        tgam = A.op(lambda e: e.activation(st[:, 4:7], st[:, 4:7], ACT.Exp, scale=-DECAY_C), t)
        t = V.op(lambda e: e.tensor_tensor(Sx[:, :], S_[:, :], sg[:, :], ALU.subtract), Sx.free)
        E2 = sg
        t1 = A.op(lambda e: e.activation(Sx[:, :], Sx[:, :], ACT.Exp, scale=-DECAY_C), t)
        t2 = A.op(lambda e: e.activation(E2[:, :], S_[:, :], ACT.Exp, scale=DECAY_C))
        t3 = A.op(lambda e: e.activation(S_[:, :], S_[:, :], ACT.Exp, scale=-DECAY_C))
        tE = [t1, t2, t3]
        yield
        kk = pool.get()
        t = V.op(lambda e: e.tensor_scalar(kk[:, :], k_[:, :], PV("k_k", i), None, ALU.mult), kk.free, tk)
        t = A.op(lambda e: e.activation(tmp[:, :], kk[:, :], ACT.Square), t, tg)
        b = psum.get()
        t = PE.many([mm(b[:, :], C("blk"), tmp[:, :], True, True)], t, b.free)
        t = V.op(lambda e: e.tensor_scalar(tmp[:, :], b[:, :], 1e-24, None, ALU.max), t)
        psum.put(b, t)
        t = A.op(lambda e: e.activation(tmp[:, :], tmp[:, :], ACT.Sqrt), t)
        t = V.op(lambda e: e.reciprocal(tmp[:, :], tmp[:, :]), t)
        t = V.op(lambda e: e.tensor_tensor(kk[:, :], kk[:, :], tmp[:, :], ALU.mult))
        t = V.op(lambda e: e.tensor_scalar(tmp[:, :], a_[:, :], 1.0, PV("k_a", i), ALU.subtract, ALU.mult), ta)
        t = V.op(lambda e: e.scalar_tensor_tensor(out=k_[:, :], in0=tmp[:, :], scalar=1.0, in1=k_[:, :],
                                                  op0=ALU.add, op1=ALU.mult))
        t = V.op(lambda e: e.tensor_tensor(a_[:, :], a_[:, :], kk[:, :], ALU.mult))
        yield
        r_ = pool.get()
        tr_ = shifted(1 + i, i, r_[:, :], r_.free)
        kr0, kr1 = pool.get(), pool.get()

        def KR(c, which=None):
            base = (kr0, kr1)[c // 2]
            o = (c % 2) * 256
            return base[:, o:o + 256] if which is None else base[:, o + which * 128:o + which * 128 + 128]

        for half, base in enumerate((kr0, kr1)):
            v4 = base.ap.rearrange("p (c w q) -> p c w q", c=2, w=2)
            sl = slice(half * 256, half * 256 + 256)
            t = V.op(lambda e, v4=v4, sl=sl: e.tensor_tensor(v4[:, :, 0, :], r3(kk[:, sl], 2), r3(Sx[:, sl], 2),
                                                             ALU.mult), base.free, tE)
            t = V.op(lambda e, v4=v4, sl=sl: e.tensor_tensor(v4[:, :, 1, :], r3(r_[:, sl], 2), r3(S_[:, sl], 2),
                                                             ALU.mult))
        t = V.op(lambda e: e.scalar_tensor_tensor(out=tmp[:, :], in0=r_[:, :], scalar=PV("r_k", i), in1=k_[:, :],
                                                  op0=ALU.mult, op1=ALU.mult))
        bb = psum.get()
        tb = PE.many([mm(bb[:, :], C("blk"), tmp[:, :], True, True)], t, bb.free)
        pool.put(Sx, t)
        pool.put(S_, t)
        pool.put(kk, t)
        kh = V.op(lambda e: e.tensor_tensor(k_[:, :], k_[:, :], E2[:, :], ALU.mult))
        tbh = V.op(lambda e: e.tensor_tensor(a_[:, :], a_[:, :], E2[:, :], ALU.mult))
        pool.put(sg, tbh)
        v_ = pool.get()
        tv = shifted(9 + i, 8 + i, v_[:, :], v_.free)
        yield
        toks = []
        vt, kt, bt = pool.get(), pool.get(), pool.get()
        for src, dst, sc, ts in ((v_, vt, 1.0, tv), (k_, kt, 1.0, kh), (a_, bt, -1.0, tbh)):
            b = psum.get()
            t = PE.many([tr(b[:, c * 128:c * 128 + 128], src[:, c * 128:c * 128 + 128]) for c in range(4)], ts,
                        b.free)
            t = A.op(lambda e, dst=dst, b=b, sc=sc: e.activation(dst[:, :], b[:, :], ACT.Copy, scale=sc), t,
                     dst.free)
            psum.put(b, t)
            toks.append(t)
        ttok = list(toks)
        tbon = V.op(lambda e: e.tensor_tensor(v_[:, :], v_[:, :], bb[:, :], ALU.mult), tb, ttok)
        psum.put(bb, tbon)
        tkr = tbon
        yield
        yt = r_
        M = pool.get()
        tM = None
        prev_reads = []
        for c in range(4):
            cs = slice(c * 128, c * 128 + 128)
            S4 = [pool.get(), pool.get()]
            tS = []
            TX = pool.get()
            for h in range(2):
                hp = slice(h * 64, h * 64 + 64)
                b = psum.get()
                t = PE.many([mm(b[:, 0:256], k_[hp, cs], KR(c)[hp, :], True, True),
                             mm(b[:, 256:512], a_[hp, cs], KR(c)[hp, :], False, True)], tkr, b.free)
                t = V.op(lambda e, h=h, b=b, S4=S4: e.tensor_tensor(S4[h][:, :], b[:, :], sh.m512[:, :], ALU.mult),
                         t, S4[h].free, sh.tm)
                psum.put(b, t)
                tS.append(t)
            bs = [psum.get(), psum.get()]
            t = PE.many([mm(bs[h][:, 0:128], KR(c, 0)[h * 64:h * 64 + 64, :], a_[h * 64:h * 64 + 64, cs], True, True)
                         for h in range(2)], tkr, bs[0].free, bs[1].free)
            for h in range(2):
                t = V.op(lambda e: e.tensor_tensor(TX[:, h * 128:h * 128 + 128], bs[h][:, 0:128], sh.lm(7), ALU.mult),
                         t, TX.free, sh.tm)
                psum.put(bs[h], t)
                t = V.op(lambda e, h=h, TX=TX, S4=S4: e.tensor_tensor(
                    TX[:, 256 + h * 128:384 + h * 128], S4[h][:, 256:384], sh.lm(0), ALU.mult), t)
            for q in range(4):
                t = V.op(lambda e, q=q, TX=TX: e.tensor_tensor(TX[:, q * 128:q * 128 + 128],
                                                               TX[:, q * 128:q * 128 + 128], C("ident"), ALU.add))
            tTX = t
            yield
            NZ = [pool.get(), pool.get()]
            for l in range(1, 7):
                nz = NZ[l % 2]
                for h in range(2):
                    tn = G.op(lambda e, h=h, l=l, nz=nz, S4=S4: e.tensor_tensor(
                        nz[:, h * 128:h * 128 + 128], S4[h][:, 256:384], sh.lm(l), ALU.mult), tS, nz.free, sh.tm)
                b = psum.get()
                t = PE.many([mm(b[:, h * 128:h * 128 + 128], nz[:, h * 128:h * 128 + 128],
                                TX[:, h * 128:h * 128 + 128], h == 0, True) for h in range(2)], tn, tTX, b.free)
                t = A.op(lambda e, nz=nz, b=b: e.activation(nz[:, 256:512], b[:, 0:256], ACT.Copy), t)
                psum.put(b, t)
                yield
                b = psum.get()
                fns = []
                if l < 6:
                    fns += [mm(b[:, h * 128:h * 128 + 128], TX[:, 256 + h * 128:384 + h * 128],
                               nz[:, 256 + h * 128:384 + h * 128], h == 0, True) for h in range(2)]
                fns += [mm(b[:, 256 + h * 128:384 + h * 128], nz[:, 256 + h * 128:384 + h * 128],
                           TX[:, 256 + h * 128:384 + h * 128], h == 0 and l == 6, True) for h in range(2)]
                t = PE.many(fns, t, b.free)
                nz.free = [t]
                o = 0 if l < 6 else 256
                tTX = V.op(lambda e, b=b, TX=TX, o=o: e.tensor_tensor(TX[:, o:512], TX[:, o:512], b[:, o:512],
                                                                      ALU.add), t)
                psum.put(b, tTX)
                yield
            for nz in NZ:
                pool.put(nz, nz.free)
            b = psum.get()
            fns = []
            if c:
                fns.append(mm(b[:, 0:128], KR(c, 0), M[:, 0:128], True, False))
            fns += [mm(b[:, h * 64:h * 64 + 64], S4[h][:, 0:128], vt[:, c * 128 + h * 64:c * 128 + h * 64 + 64],
                       not c and h == 0, True) for h in range(2)]
            t = PE.many(fns, tS, tM, ttok, b.free)
            t = A.op(lambda e, b=b: e.activation(M[:, 256:384], b[:, 0:128], ACT.Copy), t, M.free)
            psum.put(b, t)
            yield
            b = psum.get()
            t = PE.many([mm(b[:, h * 64:h * 64 + 64], TX[:, 256 + h * 128:384 + h * 128],
                            M[:, 256 + h * 64:320 + h * 64], h == 0, True) for h in range(2)], t, tTX, b.free)
            pool.put(TX, t)
            t = A.op(lambda e, b=b: e.activation(M[:, 384:512], b[:, 0:128], ACT.Copy), t)
            psum.put(b, t)
            yield
            b = psum.get()
            fns = []
            for h in range(2):
                o = b[h * 64:h * 64 + 64, 0:128]
                if c:
                    fns.append(mm(o, M[:, h * 64:h * 64 + 64], KR(c, 1), True, False))
                fns.append(mm(o, vt[:, c * 128 + h * 64:c * 128 + h * 64 + 64], S4[h][:, 128:256], not c, False))
                fns.append(mm(o, M[:, 384 + h * 64:448 + h * 64], S4[h][:, 384:512], False, True))
            ty = PE.many(fns, t, b.free)
            t2 = A.op(lambda e, b=b, cs=cs: e.activation(yt[:, cs], b[:, 0:128], ACT.Copy), ty, tkr)
            psum.put(b, t2)
            tyt = t2
            if c < 3:
                b = psum.get()
                t = PE.many([mm(b[:, 0:128], kt[:, cs], vt[:, cs], True, False),
                             mm(b[:, 0:128], bt[:, cs], M[:, 384:512], False, True)], b.free)
                if c:
                    t = V.op(lambda e, b=b: e.tensor_tensor(M[:, 128:256], M[:, 0:128], b[:, 0:128], ALU.add), t)
                    tM = V.op(lambda e, c=c: e.scalar_tensor_tensor(
                        out=M[:, 0:128], in0=M[:, 128:256], scalar=st[:, 4 + c:5 + c], in1=C("blk"), op0=ALU.mult,
                        op1=ALU.mult), tgam)
                    psum.put(b, t)
                else:
                    tM = V.op(lambda e, b=b, c=c: e.scalar_tensor_tensor(
                        out=M[:, 0:128], in0=b[:, 0:128], scalar=st[:, 4 + c:5 + c], in1=C("blk"), op0=ALU.mult,
                        op1=ALU.mult), t, tgam, M.free)
                    psum.put(b, tM)
                ty = t
            for x in S4:
                pool.put(x, ty)
            yield
        for x in (M, kr0, kr1, vt, kt, bt, k_, a_):
            pool.put(x, ty, tM, tyt)
        stats.put(st, tM)
        b = psum.get()
        t = PE.many([mm(b[:, :], C("blk"), yt[:, :], True, True)], tyt, b.free)
        t = V.op(lambda e: e.scalar_tensor_tensor(out=yt[:, :], in0=b[:, :], scalar=-1.0 / 64, in1=yt[:, :],
                                                  op0=ALU.mult, op1=ALU.add), t)
        psum.put(b, t)
        t = A.op(lambda e: e.activation(tmp[:, :], yt[:, :], ACT.Square), t)
        b = psum.get()
        t = PE.many([mm(b[:, :], C("blk"), tmp[:, :], True, True)], t, b.free)
        yield
        t1, t2 = rsqrt(tmp[:, :], b[:, :], 1.0 / 64, PV("gneps"), t)
        psum.put(b, t1)
        t = V.op(lambda e: e.scalar_tensor_tensor(out=yt[:, :], in0=yt[:, :], scalar=PV("ln_w", i), in1=tmp[:, :],
                                                  op0=ALU.mult, op1=ALU.mult), t2)
        t = V.op(lambda e: e.scalar_tensor_tensor(out=yt[:, :], in0=yt[:, :], scalar=PV("ln_b", i), in1=v_[:, :],
                                                  op0=ALU.add, op1=ALU.add), tbon)
        t = V.op(lambda e: e.tensor_tensor(yt[:, :], yt[:, :], g_[:, :], ALU.mult))
        Y[i] = (yt, t)
        for x in (tmp, g_, v_):
            pool.put(x, t)
        yield

    def roped(src, tsrc, dst, dfree, rot, cos, sin, tcs):
        b = psum.get()
        t = PE.many([mm(b[:, :], C(rot), src, True, True)], tsrc, b.free)
        t1 = V.op(lambda e: e.tensor_tensor(dst, src, cos, ALU.mult), tsrc, tcs, dfree)
        tmp = pool.get()
        t2 = V.op(lambda e: e.tensor_tensor(tmp[:, :], b[:, :], sin, ALU.mult), t, tmp.free)
        psum.put(b, t2)
        t3 = V.op(lambda e: e.tensor_tensor(dst, dst, tmp[:, :], ALU.add))
        pool.put(tmp, t3)
        return [t, t3]

    def pv_out(bank, row, vparts, PT, nj, causal, tv, first, last):
        fns = []
        PT3 = r3(PT.ap, 4)
        for j in range(nj):
            q0 = j * 128 if causal else 0
            vp = vparts(j)
            kp = vp.shape[0]
            fns.append(mm(bank[row:row + vp.shape[1], q0:T], vp, PT3[0:kp, j, q0:T], first and j == 0,
                          last and j == nj - 1))
        return fns

    def nsa(nm):
        q, qr = [pool.get(), pool.get()], [pool.get(), pool.get()]
        cos, sin = pool.get(), pool.get()
        tcs = [load(cos[:, :], dram["nsa_cos"], "ncs", cos.free), load(sin[:, :], dram["nsa_sin"], "ncs", sin.free)]
        kcv = pool.get()
        ks, kw = pool.get(), pool.get()
        vsw = pool.get()
        tkcv = proj_fm(nm, "w_in", 23, kcv[:, :], kcv.free)
        yield
        w1 = ptp.get()
        tw = load(w1[:, :], dram["cmp_w1"], "w1", w1.free)
        w2 = pool.get()
        tw2 = load(w2[0:64, 0:192], dram["cmp_w2"], "w1", w2.free)
        w13 = w1.ap.rearrange("p (j e) -> p j e", j=32)
        hs = []
        for z in range(2):
            pp = slice(z * 64, z * 64 + 64)
            b = psum.get()
            fns = []
            for j in range(32):
                fns.append(mm(b[0:64, 0:31], w13[pp, j, :], kcv[pp, j:j + 16 * 30 + 1:16], j == 0, j == 31))
            for j in range(32):
                fns.append(mm(b[0:64, 32:33], w13[pp, j, :], PV("pos", j)[pp, :], False, j == 31))
            t = PE.many(fns, tkcv, tw, tw2, b.free)
            h_ = stats.get()
            t = V.op(lambda e, b=b, h_=h_: e.tensor_copy(h_[0:64, 64:65], b[0:64, 32:33]), t, h_.free)
            t = V.op(lambda e, b=b, h_=h_: e.tensor_scalar(h_[0:64, 0:31], b[0:64, 0:31], h_[0:64, 64:65], None,
                                                           ALU.add))
            psum.put(b, t)
            t = A.op(lambda e, h_=h_: e.activation(h_[0:64, 32:63], h_[0:64, 0:31], ACT.Tanh, scale=0.5), t)
            t = V.op(lambda e, h_=h_: e.tensor_scalar(h_[0:64, 32:63], h_[0:64, 32:63], 1.0, 0.5, ALU.add,
                                                      ALU.mult), t)
            t = V.op(lambda e, h_=h_: e.tensor_tensor(h_[0:64, 0:31], h_[0:64, 0:31], h_[0:64, 32:63], ALU.mult))
            hs.append((h_, t))
            yield
        b = psum.get()
        t = PE.many([mm(b[:, 0:31], w2[0:64, 0:128], hs[0][0][0:64, 0:31], True, True),
                     mm(b[0:31, 64:128], hs[1][0][0:64, 0:31], w2[0:64, 128:192], False, True)], hs[0][1],
                    hs[1][1], b.free)
        kc, vc = stats.get(), stats.get()
        t1 = V.op(lambda e: e.tensor_copy(kc[:, 0:31], b[:, 0:31]), t, kc.free)
        tkc = V.op(lambda e: e.tensor_copy(vc[0:31, 0:64], b[0:31, 64:128]), vc.free)
        psum.put(b, tkc)
        ptp.put(w1, t)
        pool.put(kcv, t)
        pool.put(w2, t)
        stats.put(hs[0][0], t)
        stats.put(hs[1][0], t)
        for z in range(2):
            t = proj_fm(nm, "w_in", 17 + z, q[z][:, :], q[z].free)
            q[z].tok = t
            q[z].rt = qr[z].rt = roped(q[z][:, :], t, qr[z][:, :], qr[z].free, "rot_n", cos[:, :], sin[:, :], tcs)
            yield
        for u, k_ in ((24, ks), (25, kw)):
            t = proj_fm(nm, "w_in", u, k_[:, :], k_.free)
            k_.rt = roped_inplace(k_, t, "rot_n", cos, sin, tcs)
            yield
        pool.put(cos, kw.rt)
        pool.put(sin, kw.rt)
        vs3 = r3(vsw.ap, 4)
        tv, _ = proj_tm(nm, "w_in", 26, vs3, vsw.free)
        yield
        w = weight("w_in", 0)
        gl = stats.get()
        gl3 = gl.ap[:, 0:48].rearrange("p (t c) -> p t c", t=4)
        tgl, tlast = proj_tm(nm, "w_in", 0, gl3, gl.free, m=(0, 12), w_=w)
        drop(w[0], tlast)
        for tt in range(4):
            t = V.op(lambda e, tt=tt: e.tensor_tensor(gl3[:, tt, :], gl3[:, tt, :], PV("gate_b", 0, 12), ALU.add),
                     tgl)
        t = A.op(lambda e: e.activation(gl[:, 0:48], gl[:, 0:48], ACT.Tanh, scale=0.5), t)
        tgl = V.op(lambda e: e.tensor_scalar(gl[:, 0:48], gl[:, 0:48], 1.0, 0.5, ALU.add, ALU.mult), t)
        yield
        cp, cm = pool.get(), pool.get()
        tcm = load(cm[:, 0:256], dram["cmp_mask"], "cmask", cm.free)
        bs = [psum.get(), psum.get()]
        fns = []
        for h in range(4):
            hp = slice((h % 2) * 64, (h % 2) * 64 + 64)
            for i in range(4):
                o = (h * 4 + i) * 32
                fns.append(mm(bs[h % 2][:, o:o + 31], q[h // 2][hp, i * 128:i * 128 + 128], kc[hp, 0:31],
                              h < 2 and i == 0, True))
        t = PE.many(fns, tkc, q[0].tok, q[1].tok, bs[0].free, bs[1].free)
        bv = [b.ap.rearrange("p (g c) -> p g c", g=16)[:, :, 0:31] for b in bs]
        cp3 = cp.ap.rearrange("p (g c) -> p g c", g=16)[:, :, 0:31]
        cma = r3(cm[:, 0:128], 4)[:, :, 0:31]
        cmm = r3(cm[:, 128:256], 4)[:, :, 0:31]
        for h in range(4):
            t = V.op(lambda e, h=h: e.tensor_tensor(cp3[:, h * 4:h * 4 + 4, :], bv[h % 2][:, h * 4:h * 4 + 4, :],
                                                    cma, ALU.add), t, tcm, cp.free)
        for b in bs:
            psum.put(b, t)
        sc = stats.get()
        t = V.op(lambda e: e.tensor_reduce(sc[:, 0:16], cp3, AX, ALU.max), sc.free)
        t = V.op(lambda e: e.tensor_tensor(cp3, cp3, sc[:, 0:16].unsqueeze(2).to_broadcast([128, 16, 31]),
                                           ALU.subtract))
        t = A.op(lambda e: e.activation(cp3, cp3, ACT.Exp, scale=0.125), t)
        for h in range(4):
            t = V.op(lambda e, h=h: e.tensor_tensor(cp3[:, h * 4:h * 4 + 4, :], cp3[:, h * 4:h * 4 + 4, :], cmm,
                                                    ALU.mult), t)
        t = V.op(lambda e: e.tensor_reduce(sc[:, 16:32], cp3, AX, ALU.add))
        t = V.op(lambda e: e.tensor_scalar(sc[:, 16:32], sc[:, 16:32], 1e-30, None, ALU.max))
        t = V.op(lambda e: e.reciprocal(sc[:, 16:32], sc[:, 16:32]))
        gl4 = gl.ap[:, 0:48].rearrange("p (t h b) -> p h t b", t=4, h=4)
        t = V.op(lambda e: e.tensor_tensor(r3(sc[:, 32:48], 4), r3(sc[:, 16:32], 4), gl4[:, :, :, 0], ALU.mult))
        tcp = V.op(lambda e: e.tensor_tensor(cp3, cp3, sc[:, 32:48].unsqueeze(2).to_broadcast([128, 16, 31]),
                                             ALU.mult))
        stats.put(sc, tcp)
        pool.put(cm, tcp)
        for x in q:
            pool.put(x, t, x.rt, tkc)
        stats.put(kc, t)
        yield
        oT = [pool.get(), pool.get()]
        gt = pool.get()
        for z in range(2):
            ob = psum.get()
            for hh in range(2):
                h = 2 * z + hh
                hp = slice(hh * 64, hh * 64 + 64)
                b = psum.get()
                t = PE.many([tr(b[0:31, i * 128:i * 128 + 128], cp3[:, h * 4 + i, :]) for i in range(4)], tcp,
                            b.free)
                pt = ptp.get()
                tpt = A.op(lambda e, b=b, pt=pt: e.activation(pt[0:31, 0:T], b[0:31, :], ACT.Copy), t, pt.free)
                psum.put(b, tpt)
                ob_first = PE.many([mm(ob[hh * 64:hh * 64 + 64, :], vc[0:31, 0:64], pt[0:31, 0:T], True, False)],
                                   tpt, tkc, ob.free)
                ptp.put(pt, ob_first)
                yield
                for br, (k_, vo) in enumerate(((ks, 0), (kw, 64))):
                    pt = ptp.get()
                    yield from attn_head(
                        lambda i, k_=k_, h=h, hp=hp: ([(qr[h // 2][hp, i * 128:i * 128 + 128],
                                                        k_[hp, 0:(i + 1) * 128])], [qr[h // 2].rt, k_.rt]),
                        [128, 256, 384, 512], 0.125, pt, pt.free, diag=(C("causal"), None),
                        gate=lambda i, h=h, br=br: (gl3[:, i, h * 3 + 1 + br:h * 3 + 2 + br], tgl))
                    t = PE.many(pv_out(ob, hh * 64, lambda j, vo=vo: vs3[:, j, vo:vo + 64], pt, 4, True, None,
                                       False, br == 1), pt.tok, tv)
                    ptp.put(pt, t)
                    yield
            to = V.op(lambda e, z=z, ob=ob: e.tensor_copy(oT[z][:, :], ob[:, :]), t, oT[z].free)
            psum.put(ob, to)
            t = proj_fm(nm, "w_in", 19 + z, gt[:, :], gt.free)
            tmp = pool.get()
            t = silu(gt[:, :], gt[:, :], tmp[:, :], t, tmp.free)
            t = block_norm(oT[z][:, :], [to, t], PV("nsa_out_g", z), oT[z][:, :], gt[:, :])
            pool.put(tmp, t)
            gt.free = [t]
            Y[4 + z] = (oT[z], t)
            yield
        pool.put(gt, t)
        for x in qr + [ks, kw, vsw, cp]:
            pool.put(x, t)
        stats.put(gl, t)
        stats.put(vc, t)

    def roped_inplace(k_, t, rot, cos, sin, tcs):
        b = psum.get()
        t1 = PE.many([mm(b[:, :], C(rot), k_[:, :], True, True)], t, b.free)
        t2 = V.op(lambda e: e.tensor_tensor(k_[:, :], k_[:, :], cos[:, :], ALU.mult), t1, tcs)
        tmp = pool.get()
        t2 = V.op(lambda e: e.tensor_tensor(tmp[:, :], b[:, :], sin[:, :], ALU.mult), tmp.free)
        psum.put(b, t2)
        t3 = V.op(lambda e: e.tensor_tensor(k_[:, :], k_[:, :], tmp[:, :], ALU.add))
        pool.put(tmp, t3)
        return t3

    def mem_heads(nm, mk):
        gt = pool.get()
        for z in range(2):
            q = pool.get()
            tq = proj_fm(nm, "w_in", (21, 22)[z], q[:, :], q.free)
            yield
            ob = psum.get()
            for hh in range(2):
                h = 2 * z + hh
                hp = slice(hh * 64, hh * 64 + 64)
                pt = ptp.get()
                yield from attn_head(lambda i: ([(q[hp, i * 128:i * 128 + 128], mk.kap[z][hp, :])], [tq, mk.tk]),
                                     [256] * 4, 0.125, pt, pt.free)
                t = PE.many(pv_out(ob, hh * 64, lambda j: mk.vap(j, h * 64, h * 64 + 64), pt, 2, False, None, True,
                                   True), pt.tok, mk.tv, ob.free)
                ptp.put(pt, t)
            pool.put(q, t)
            o = pool.get()
            to = V.op(lambda e: e.tensor_copy(o[:, :], ob[:, :]), t, o.free)
            psum.put(ob, to)
            t = proj_fm(nm, "w_in", 27 + z, gt[:, :], gt.free)
            tmp = pool.get()
            t = silu(gt[:, :], gt[:, :], tmp[:, :], t, tmp.free)
            t = block_norm(o[:, :], [to, t], PV("mem_out_g", z), o[:, :], gt[:, :])
            pool.put(tmp, t)
            gt.free = [t]
            Y[6 + z] = (o, t)
            yield
        pool.put(gt, t)
        for x in mk.kts + mk.vts:
            pool.put(x, t)

    omm, w0h, a0h = env.omm[:, 0:17], env.omm[:, 17:21], env.omm[:, 21:25]
    V.op(lambda e: e.tensor_scalar(omm, PV("mu", 0, 17), -1.0, 1.0, ALU.mult, ALU.add))
    V.op(lambda e: e.tensor_scalar(w0h, PV("w0", 0, 4), 0.5, None, ALU.mult))
    t_omm = V.op(lambda e: e.tensor_scalar(a0h, PV("a0h", 0, 4), 0.5, None, ALU.mult))

    m_hi, m_lo = mem_pairs()
    mk = mem_act("memT", "mem_norm_g", m_hi, m_lo)
    nm = norm_input("norm_in_g", True)
    drive(mem_kv(mk, "w_mem_kv", 2, m_hi, m_lo))
    to_pool()
    sh = Norm()
    sh.m512, lm2, sh.lora = pool.get(), [pool.get(), pool.get()], pool.get()
    t = [load(sh.m512[:, :], dram["m512"], "rm", sh.m512.free), load(lm2[0][:, :], dram["lm"][0], "rm", lm2[0].free),
         load(lm2[1][:, :], dram["lm"][1], "rm", lm2[1].free), load(sh.lora[:, :], dram["lora"], "rm", sh.lora.free)]
    sh.tm = t[-1]
    sh.lm = lambda l: lm2[l // 4][:, (l % 4) * 128:(l % 4) * 128 + 128]
    sh.wdad = pool.get()
    rt = pool.get()
    w_, wt_ = weight("w_in", 29)
    b = psum.get()
    t = PE.many(fm(b, w_, ahi, alo, ND), wt_, nm.act, b.free)
    drop(w_, t)
    t = V.op(lambda e, b=b: e.tensor_tensor(rt[:, :], b[:, :], nm.R[:, :], ALU.mult), t, nm.tR, rt.free)
    psum.put(b, t)
    t = V.op(lambda e: e.tensor_scalar(sh.wdad[:, :], rt[:, :], omm[:, 16:17], None, ALU.mult), sh.wdad.free)
    t = V.op(lambda e: e.scalar_tensor_tensor(out=sh.wdad[:, 1:T], in0=rt[:, 0:T - 1], scalar=PV("mu", 16),
                                              in1=sh.wdad[:, 1:T], op0=ALU.mult, op1=ALU.add))
    pool.put(rt, t)
    t = A.op(lambda e: e.activation(sh.wdad[0:64, :], sh.wdad[0:64, :], ACT.Tanh), t)
    sh.tl = [t, sh.tm]

    def nsa_then_mem():
        yield from nsa(nm)
        yield from mem_heads(nm, mk)

    drive(par([par([rwkv_pair(nm, i, sh) for i in range(4)], env.rw), nsa_then_mem()], 2))
    for x in (sh.m512, lm2[0], lm2[1], sh.lora, sh.wdad):
        pool.put(x, Y[3][1], (PE.sem, PE.count), (G.sem, G.count))

    def finish_mix(nm, name):
        pool.put(nm.R, (V.sem, V.count))
        stats.put(nm.col, (A.sem, A.count))
        for i in range(ND):
            yb, ty = Y[i]
            t1, t2 = split_plain(yb[:, :], ahi[i][:, :], alo[i][:, :], ty, nm.last)
            pool.put(yb, t1, t2)
            ahi[i].tok, alo[i].tok = t1, t2
        drive(residual_dense(name, ahi, alo, [[a.tok for a in ahi], [a.tok for a in alo]]))

    finish_mix(nm, "w_out")

    def final_norm(gname):
        acc = pool.get()
        nonlocal acc_free
        acc_free = acc.free
        t = squares([(X[i][:, :], X[i].tok) for i in range(ND)], T, acc.ap)
        nm = stats_of(acc.ap, T, t, 1024, False)
        pool.put(acc, nm.t_acc_read)
        for i in range(ND):
            X[i].tok = V.op(lambda e, i=i: e.scalar_tensor_tensor(
                out=X[i][:, :], in0=X[i][:, :], scalar=PV(gname, i), in1=nm.R[:, :], op0=ALU.mult, op1=ALU.mult),
                nm.tR, X[i].tok, t)
        pool.put(nm.R, X[7].tok)

    final_norm("norm_final_g")

    def diff_head(nm, h, sd):
        q, k, v = pool.get(), pool.get(), pool.get()
        tq = proj_fm(nm, "ev_w_in", h, q[:, :], q.free)
        yield
        tk = proj_fm(nm, "ev_w_in", 4 + h, k[:, :], k.free)
        yield
        v3 = r3(v.ap, 4)
        tv, _ = proj_tm(nm, "ev_w_in", 8 + h, v3, v.free)
        yield
        slope = 2.0 ** (-8.0 * (h + 1) / 4)
        pt = ptp.get()
        PT3 = r3(pt.ap, 4)
        outs = []
        for i in range(4):
            nk = (i + 1) * 128
            prs, sts = [], []
            st = stats.get()
            for z in range(2):
                hp = slice(z * 64, z * 64 + 64)
                b = psum.get()
                t = PE.many([mm(b[:, 0:nk], q[hp, i * 128:i * 128 + 128], k[hp, 0:nk], True, True)], tq, tk, b.free)
                t = V.op(lambda e, b=b, nk=nk, i=i: e.scalar_tensor_tensor(
                    out=b[:, 0:nk], in0=sd.dist(i), scalar=slope * 8.0, in1=b[:, 0:nk], op0=ALU.mult,
                    op1=ALU.add), t, sd.td)
                o = z * 4
                t = V.op(lambda e, b=b, nk=nk, o=o, st=st: e.tensor_reduce(st[:, o:o + 1], b[:, 0:nk], AX, ALU.max),
                         st.free)
                t = V.op(lambda e, o=o, st=st: e.tensor_scalar(st[:, o + 1:o + 2], st[:, o:o + 1], -0.125, None,
                                                               ALU.mult))
                pr = pool.get()
                t = A.op(lambda e, b=b, nk=nk, o=o, st=st, pr=pr: e.activation(
                    pr[:, 0:nk], b[:, 0:nk], ACT.Exp, bias=st[:, o + 1:o + 2], scale=0.125,
                    accum_out=st[:, o + 2:o + 3]), t, pr.free)
                psum.put(b, t)
                t = V.op(lambda e, o=o, st=st: e.reciprocal(st[:, o + 3:o + 4], st[:, o + 2:o + 3]), t)
                prs.append(pr)
                yield
            t = V.op(lambda e, st=st: e.tensor_tensor(st[:, 7:8], st[:, 7:8], sd.nlam[:, 0:1], ALU.mult), sd.tlam)
            t = V.op(lambda e, st=st, nk=nk, prs=prs: e.tensor_scalar(prs[0][:, 0:nk], prs[0][:, 0:nk], st[:, 3:4],
                                                                      None, ALU.mult))
            t = V.op(lambda e, st=st, nk=nk, prs=prs: e.scalar_tensor_tensor(
                out=prs[0][:, 0:nk], in0=prs[1][:, 0:nk], scalar=st[:, 7:8], in1=prs[0][:, 0:nk], op0=ALU.mult,
                op1=ALU.add))
            stats.put(st, t)
            pool.put(prs[1], t)
            yield
            tt, t2 = turn(prs[0], nk, i, PT3, t, pt.free)
            pool.put(prs[0], tt)
            outs.append(t2)
            yield
        ob = psum.get()
        pool.put(q, tt)
        pool.put(k, tt)
        t = PE.many(pv_out(ob, 0, lambda j: v3[:, j, :], pt, 4, True, None, True, True), outs, tv, ob.free)
        ptp.put(pt, t)
        pool.put(v, t)
        o_, sq = pool.get(), pool.get()
        to = V.op(lambda e: e.tensor_copy(o_[:, :], ob[:, :]), t, o_.free)
        psum.put(ob, to)
        t = A.op(lambda e: e.activation(sq[:, :], o_[:, :], ACT.Square), to, sq.free)
        b = psum.get()
        t = PE.many([mm(b[:, :], C("ones"), sq[:, :], True, True)], t, b.free)
        yield
        t1, t2 = rsqrt(sq[:, :], b[:, :], 1.0 / 128, PV("eps6"), t)
        psum.put(b, t1)
        t = V.op(lambda e: e.scalar_tensor_tensor(out=o_[:, :], in0=o_[:, :], scalar=sd.sub[:, 0:1], in1=sq[:, :],
                                                  op0=ALU.mult, op1=ALU.mult), t2, sd.tlam)
        pool.put(sq, t)
        Y[h] = (o_, t)
        yield

    def mla(nm, sd):
        cos, sin = pool.get(), pool.get()
        tcs = [load(cos[:, :], dram["mla_cos"], "mcs", cos.free), load(sin[:, :], dram["mla_sin"], "mcs", sin.free)]
        kr = pool.get()
        t = proj_fm(nm, "ev_w_in", 15, kr[:, :], kr.free)
        tkr = roped_inplace(kr, t, "rot_m", cos, sin, tcs)
        yield
        ws = sd.lowrank
        toks = []

        def low(units, gname, dsts, d):
            cs = [pool.get() for _ in units]
            ts = []
            for c_, u in zip(cs, units):
                ts.append(proj_fm(nm, "ev_w_in", u, c_[:, :], c_.free))
            acc = pool.get()
            sq = pool.get()
            t = A.op(lambda e: e.activation(acc[:, :], cs[0][:, :], ACT.Square), ts[0], acc.free)
            if len(cs) > 1:
                t = A.op(lambda e: e.activation(sq[:, :], cs[1][:, :], ACT.Square), ts[1], sq.free)
                t = V.op(lambda e: e.tensor_tensor(acc[:, :], acc[:, :], sq[:, :], ALU.add), t)
            pool.put(sq, t)
            s_ = stats_of(acc.ap, T, t, d, False)
            pool.put(acc, s_.t_acc_read)
            res = []
            for n, c_ in enumerate(cs):
                t = V.op(lambda e, n=n, c_=c_: e.scalar_tensor_tensor(
                    out=c_[:, :], in0=c_[:, :], scalar=PV(gname, n), in1=s_.R[:, :], op0=ALU.mult, op1=ALU.mult),
                    s_.tR)
                t1, t2 = split_plain(c_[:, :], dsts[n][0][:, :], dsts[n][1][:, :], t, dsts[n][0].free)
                pool.put(c_, t1, t2)
                res += [t1, t2]
            pool.put(s_.R, t)
            return res

        hq, hk = [(hhi[0], hlo[0]), (hhi[1], hlo[1])], [(hhi[2], hlo[2])]
        tq_ = low([12, 13], "g_cq", hq, 256)
        yield
        tkv_ = low([14], "g_ckv", hk, 128)
        yield
        qn, qrp = [pool.get() for _ in range(4)], [pool.get(), pool.get()]
        qt = []
        wq, wqt = None, None
        for mtl in range(6):
            if mtl % 4 == 0:
                if wq is not None:
                    drop(wq, t)
                wq, wqt = weight("uq", mtl // 4)
            b = psum.get()
            t = PE.many(fm(b, wq, [x[0] for x in hq], [x[1] for x in hq], 2, wk=(mtl % 4) * 2), wqt, tq_, b.free)
            dst = (qn + qrp)[mtl]
            t2 = A.op(lambda e, b=b, dst=dst: e.activation(dst[:, :], b[:, :], ACT.Copy), t, dst.free)
            psum.put(b, t2)
            qt.append(t2)
            yield
        drop(wq, t)
        for z in range(2):
            qt[4 + z] = roped_inplace(qrp[z], qt[4 + z], "rot_m", cos, sin, tcs)
            yield
        pool.put(cos, qt[5])
        pool.put(sin, qt[5])
        wk_, wkt = weight("ukv", 0)
        kn, vn = [pool.get() for _ in range(4)], [pool.get() for _ in range(4)]
        kt_, vt_ = [], []
        for h in range(4):
            b = psum.get()
            t = PE.many(fm(b, wk_, [hk[0][0]], [hk[0][1]], 1, wk=h), wkt, tkv_, b.free)
            t2 = A.op(lambda e, b=b, h=h: e.activation(kn[h][:, :], b[:, :], ACT.Copy), t, kn[h].free)
            psum.put(b, t2)
            kt_.append(t2)
            b = psum.get()
            fns = []
            for tt in range(4):
                fns += tm(b[:, tt * 128:tt * 128 + 128], wk_, [hk[0][0]], [hk[0][1]], 1, tt, tt == 0, wk=4 + h)
            t = PE.many(fns, b.free)
            t2 = A.op(lambda e, b=b, h=h: e.activation(vn[h][:, :], b[:, :], ACT.Copy), t, vn[h].free)
            psum.put(b, t2)
            vt_.append(t2)
            yield
        drop(wk_, t)
        for b_ in hhi + hlo:
            b_.free = [t]
        SC = 192.0 ** -0.5
        for h in range(4):
            hp = slice((h % 2) * 64, (h % 2) * 64 + 64)
            pt = ptp.get()
            yield from attn_head(
                lambda i: ([(qn[h][:, i * 128:i * 128 + 128], kn[h][:, 0:(i + 1) * 128]),
                            (qrp[h // 2][hp, i * 128:i * 128 + 128], kr[hp, 0:(i + 1) * 128])],
                           [qt, kt_, tkr]),
                [128, 256, 384, 512], SC, pt, pt.free, diag=(sd.cm[:, 0:128], sd.td))
            ob = psum.get()
            v3 = r3(vn[h].ap, 4)
            t = PE.many(pv_out(ob, 0, lambda j: v3[:, j, :], pt, 4, True, None, True, True), pt.tok, vt_, ob.free)
            ptp.put(pt, t)
            o_ = qn[h]
            t2 = A.op(lambda e: e.activation(o_[:, :], ob[:, :], ACT.Copy), t)
            psum.put(ob, t2)
            Y[4 + h] = (o_, t2)
            pool.put(kn[h], t)
            pool.put(vn[h], t)
            yield
        for x in qrp + [kr]:
            pool.put(x, t)

    def even_layer():
        nm = norm_input("ev_norm", True)
        sd = Norm()
        dt = [pool.get() for _ in range(3)]
        for n in range(3):
            w_ = min(512, 1280 - n * 512)
            t = load(dt[n][:, 0:w_], dram["dist"][:, n * 512:n * 512 + w_], "cs", dt[n].free)
        dmb = pool.get()
        t = load(dmb[:, 0:128], dram["cmask"], "cs", dmb.free)
        sd.td = t

        def dist(i):
            if i == 0:
                return dt[0][:, 0:128]
            if i == 2:
                return dt[0][:, 128:512]
            if i == 3:
                return dt[1][:, 0:512]
            return dt[2][:, 0:256]

        sd.dist = dist
        sd.cm = dmb
        ls = stats.get()
        l4 = PV("lqk", 0, 4)
        t = V.op(lambda e: e.tensor_tensor(ls[:, 0:2], l4[:, 0:2], l4[:, 2:4], ALU.mult), ls.free)
        b = psum.get()
        t = PE.many([mm(b[:, 0:2], C("ones")[0:64, :], ls[0:64, 0:2], True, True)], t, b.free)
        t = A.op(lambda e, b=b: e.activation(ls[:, 2:4], b[:, 0:2], ACT.Exp), t)
        psum.put(b, t)
        t = V.op(lambda e: e.tensor_tensor(ls[:, 4:5], ls[:, 3:4], ls[:, 2:3], ALU.subtract), t)
        lambda_init = 0.8 - 0.6
        t = V.op(lambda e: e.tensor_scalar(ls[:, 4:5], ls[:, 4:5], lambda_init, None, ALU.subtract))
        sd.nlam = ls[:, 4:5]
        sd.sub = ls[:, 5:6]
        sd.tlam = V.op(lambda e: e.tensor_scalar(ls[:, 5:6], PV("subln"), 1.0 - lambda_init, None, ALU.mult))
        sd.lowrank = None
        return nm, sd, dt + [dmb], ls

    to_pairs()
    to_pool((0, 1, 2))
    nm, sd, dts, ls = even_layer()

    drive(par([par([diff_head(nm, h, sd) for h in range(4)], 1), mla(nm, sd)], 2))
    for x in dts:
        pool.put(x, Y[3][1], (V.sem, V.count))
    stats.put(ls, (V.sem, V.count))
    finish_mix(nm, "ev_w_out")
    to_pairs()

    def cross(n):
        m_hi, m_lo = mem_pairs()
        mk = mem_act("mem2T", f"xa_mem{n}", m_hi, m_lo)
        nm = norm_input(f"xa_norm{n}", False)
        drive(mem_kv(mk, f"wkv{n}", 8, m_hi, m_lo))
        to_pool()

        def head(h):
            q = [pool.get(), pool.get()]
            tq = []
            for z in range(2):
                tq.append(proj_fm(nm, f"wq{n}", 2 * h + z, q[z][:, :], q[z].free))
                yield
            pt = ptp.get()
            yield from attn_head(lambda i: ([(q[z][:, i * 128:i * 128 + 128], mk.kap[2 * h + z]) for z in range(2)],
                                        [tq, mk.tk]), [256] * 4, 1.0 / 16, pt, pt.free)
            for z in range(2):
                ob = psum.get()
                c0 = (2 * h + z) * 128
                t = PE.many(pv_out(ob, 0, lambda j: mk.vap(j, c0, c0 + 128), pt, 2, False, None, True, True),
                            pt.tok, mk.tv, ob.free)
                t2 = A.op(lambda e, ob=ob, z=z: e.activation(q[z][:, :], ob[:, :], ACT.Copy), t)
                psum.put(ob, t2)
                Y[2 * h + z] = (q[z], t2)
            ptp.put(pt, t)
            yield

        drive(par([head(h) for h in range(4)], 2))
        for x in mk.kts + mk.vts:
            pool.put(x, (PE.sem, PE.count))
        pool.put(nm.R, (V.sem, V.count))
        for i in range(ND):
            yb, ty = Y[i]
            t1, t2 = split_plain(yb[:, :], ahi[i][:, :], alo[i][:, :], ty, nm.last)
            pool.put(yb, t1, t2)
            ahi[i].tok, alo[i].tok = t1, t2
        drive(residual_dense(f"wo{n}", ahi, alo, [[a.tok for a in ahi], [a.tok for a in alo]]))
        to_pairs()

    def mlp(n):
        nm = norm_input(f"mlp_norm{n}", False)
        for qd in range(4):
            ht = []
            for u in range(ND):
                w, wt = weight(f"w1{n}", qd * 8 + u)
                b = psum.get()
                t = PE.many(fm(b, w, ahi, alo, ND), wt, nm.act, b.free)
                drop(w, t)
                tmp = pool.get()
                t1 = V.op(lambda e, b=b, tmp=tmp: e.scalar_tensor_tensor(
                    out=tmp[:, :], in0=b[:, :], scalar=0.0, in1=nm.R[:, :], op0=ALU.max, op1=ALU.mult), t, nm.tR,
                    tmp.free)
                psum.put(b, t1)
                t2 = A.op(lambda e, tmp=tmp: e.activation(tmp[:, :], tmp[:, :], ACT.Square), t1)
                t3, t4 = split_plain(tmp[:, :], hhi[u][:, :], hlo[u][:, :], t2, hhi[u].free, hlo[u].free)
                pool.put(tmp, t3, t4)
                ht += [t3, t4]
            for a in ahi + alo:
                a.free = [t]
            drive(residual_dense_q(f"w2{n}", qd, ht))
        pool.put(nm.R, (V.sem, V.count))

    def residual_dense_q(name, qd, ht):
        last = None
        for u in range(ND):
            w, wt = weight(name, qd * 8 + u)
            b = psum.get()
            t = PE.many(fm(b, w, hhi, hlo, ND), wt, ht, b.free)
            drop(w, t)
            t2 = V.op(lambda e, u=u, b=b: e.tensor_tensor(X[u][:, :], X[u][:, :], b[:, :], ALU.add), t,
                      X[u].tok, X[u].reads)
            psum.put(b, t2)
            X[u].tok = t2
            last = t
            yield
        for a in hhi + hlo:
            a.free = [last]

    def sb_layer():
        nm = norm_input("od_norm", True)

        def pair(z):
            q, k, v = pool.get(), pool.get(), pool.get()
            tq = proj_fm(nm, "sb_w_in", z, q[:, :], q.free)
            tq = V.op(lambda e: e.tensor_scalar(q[:, :], q[:, :], 0.125, None, ALU.mult))
            yield
            tk = proj_fm(nm, "sb_w_in", 8 + z, k[:, :], k.free)
            yield
            v3 = r3(v.ap, 4)
            tv, _ = proj_tm(nm, "sb_w_in", 16 + z, v3, v.free)
            yield
            y = pool.get()
            ob = psum.get()
            for hh in range(2):
                hp = slice(hh * 64, hh * 64 + 64)
                sps, tsp, aws, taw = {}, {}, {}, {}
                run = None
                for j in (3, 2, 1, 0):
                    q0 = j * 128
                    n = T - q0
                    b = psum.get()
                    t = PE.many([mm(b[:, 0:n], k[hp, q0:q0 + 128], q[hp, q0:T], True, False)], tq, tk, b.free)
                    sp = pool.get()
                    t = A.op(lambda e, b=b, sp=sp, n=n: e.activation(sp[:, 0:n], b[:, 0:n], ACT.Abs), t, sp.free)
                    t = A.op(lambda e, sp=sp, n=n: e.activation(sp[:, 0:n], sp[:, 0:n], ACT.Exp, scale=-1.0))
                    t = A.op(lambda e, sp=sp, n=n: e.activation(sp[:, 0:n], sp[:, 0:n], ACT.Ln, bias=PV("one")))
                    t = V.op(lambda e, b=b, sp=sp, n=n: e.scalar_tensor_tensor(
                        out=sp[:, 0:n], in0=b[:, 0:n], scalar=0.0, in1=sp[:, 0:n], op0=ALU.max, op1=ALU.add), t)
                    t = G.op(lambda e, sp=sp: e.affine_select(
                        out=sp[:, 0:128], in_=sp[:, 0:128], compare_op=ALU.is_gt, fill=0.0, base=0,
                        pattern=[[1, 128]], channel_multiplier=-1), t)
                    sps[j], tsp[j] = sp, t
                    yield
                    fns = [mm(b[:, 0:n], C("ntri"), sp[:, 0:n], False, j == 3)]
                    if run is not None:
                        r0 = (j + 1) * 128 - q0
                        fns.append(mm(b[:, r0:n], C("nones"), run[:, 0:n - r0], False, True))
                    tpe = PE.many(fns, t, tsp.get("run"))
                    t = V.op(lambda e, b=b: e.tensor_tensor(b[:, 0:128], b[:, 0:128], C("sbm"), ALU.add), tpe)
                    aw = pool.get()
                    t2 = A.op(lambda e, b=b, aw=aw, n=n: e.activation(aw[:, 0:n], b[:, 0:n], ACT.Exp), t, aw.free)
                    psum.put(b, t2)
                    aws[j], taw[j] = aw, t2
                    if j:
                        if run is not None:
                            tr_ = V.op(lambda e, sp=sp, run=run, n=n: e.tensor_tensor(
                                sp[:, 128:n], sp[:, 128:n], run[:, 0:n - 128], ALU.add), tpe, tsp["run"])
                            pool.put(run, tpe, tr_)
                            tsp["run"] = tr_
                        else:
                            tsp["run"] = tsp[j]
                        run = sp
                    else:
                        pool.put(run, tpe)
                        pool.put(sp, tpe)
                    yield
                t = PE.many([mm(ob[hh * 64:hh * 64 + 64, j * 128:T], v3[:, j, hh * 64:hh * 64 + 64],
                                aws[j][:, 0:T - j * 128], j == 0, j == 3) for j in range(4)],
                            [taw[j] for j in range(4)], tv, ob.free)
                for j in range(4):
                    pool.put(aws[j], t)
                yield
            t2 = V.op(lambda e: e.tensor_copy(y[:, :], ob[:, :]), t, y.free)
            psum.put(ob, t2)
            Y[z] = (y, t2)
            for x in (q, k, v):
                pool.put(x, t)
            yield

        drive(par([pair(z) for z in range(8)], env.sbw))
        return nm

    cross(0)
    mlp(0)
    to_pool()
    nm = sb_layer()
    finish_mix(nm, "sb_w_out")
    to_pairs()
    cross(1)
    mlp(1)
    final_norm("final_norm")
    for i in range(ND):
        t = load(dram["outT"][i], X[i][:, :], "out", X[i].tok)
    S.wait(t)
    return seen, pool


class Env:
    pass


def build(nc, dram):
    with ExitStack() as ctx:
        def sb(name, cols, dt=F32):
            return ctx.enter_context(nc.sbuf_tensor(name, [P, cols], dt))

        env = Env()
        env.dram = dram
        env.look, env.rw, env.sbw = 2, 1, 2
        env.psum = [ctx.enter_context(nc.psum_tensor(f"ps{i}", [P, 512], F32))[:, :] for i in range(8)]
        env.cst, env.pv = sb("cst", CN), sb("pv", PN)
        env.omm = sb("omm", 32)
        env.x = [sb(f"X{i}", T)[:, :] for i in range(ND)]
        env.raw = [sb(f"raw{i}", 1024)[:, :] for i in range(4)]
        env.wr = [sb(f"wr{i}", 2048, F32R)[:, :] for i in range(3)]
        env.ahi = [sb(f"ahi{i}", T, F32R)[:, :] for i in range(ND)]
        env.alo = [sb(f"alo{i}", T, F32R)[:, :] for i in range(ND)]
        env.pt = [sb(f"pt{i}", 4 * T)[:, :] for i in range(2)]
        env.stats = [sb(f"st{i}", 66)[:, :] for i in range(12)]
        env.hhi, env.hlo, env.extra = [], [], []
        start = nc.sbuf_base
        fence = sb("fence", 16 * T)
        at = fence_address(start)
        for i in range(16):
            d = env.hhi if i < 8 else env.hlo
            d.append(nc.alloc_sbuf_tensor_at(f"h{i}", [P, T], F32R, offset=at + i * T * 4)[:, :])
            env.extra.append(nc.alloc_sbuf_tensor_at(f"e{i}", [P, T], F32, offset=at + i * T * 4)[:, :])
        n = (nc.sbuf_top - nc.sbuf_base - 64) // (T * 4)
        env.tiles = [sb(f"t{i}", T)[:, :] for i in range(n)]
        sem = lambda name: ctx.enter_context(nc.semaphore(name))
        env.sems = {k: sem("s_" + k) for k in
                    ["cst", "mem", "cs", "ncs", "mcs", "cmask", "w1", "rm", "out"] + [f"x{i}" for i in range(8)] + [f"raw{i}" for i in range(4)]}
        es = {k: sem("s_" + k) for k in ("V", "A", "G", "PE", "S")}

        def engines(real):
            def engine(name, eng, link):
                return Engine(eng if real else None, es[name], link)

            env.S, env.PE = engine("S", nc.sync, False), engine("PE", nc.tensor, False)
            env.V, env.A, env.G = engine("V", nc.vector, True), engine("A", nc.scalar, True), engine("G", nc.gpsimd, True)

        engines(False)
        order, _ = plan(env, None)
        engines(True)
        plan(env, order)


def fence_address(start):
    return (start + 31) // 32 * 32


def _constants():
    import numpy as np

    f = np.float32
    i = np.arange(128)
    a, b = i[:, None], i[None, :]
    c = {
        "ident": (a == b), "ones": np.ones((128, 128)), "blk": (a // 64 == b // 64), "ntri": -(a >= b).astype(f),
        "nones": -np.ones((128, 128)), "causal": np.where(b <= a, 0.0, NEG), "sbm": np.where(a < b, 0.0, NEG),
    }

    def rot(half):
        m = np.zeros((128, 128))
        for h in range(2):
            for x in range(half):
                m[h * 64 + half + x, h * 64 + x] = -1.0
                m[h * 64 + x, h * 64 + half + x] = 1.0
        return m

    c["rot_n"], c["rot_m"] = rot(8), rot(32)
    out = {"cst": np.concatenate([c[n].astype(f) for n, _ in CCOLS], axis=1)}

    def tables(half, base):
        inv = f(base) ** (-np.arange(half, dtype=f) / f(half))
        ang = np.arange(T, dtype=f)[None, :] * inv.astype(f)[:, None]
        cos, sin = np.ones((128, T), f), np.zeros((128, T), f)
        for h in range(2):
            for z in range(2):
                r = h * 64 + z * half
                cos[r:r + half], sin[r:r + half] = np.cos(ang), np.sin(ang)
        return cos, sin

    out["nsa_cos"], out["nsa_sin"] = tables(8, 500000.0)
    out["mla_cos"], out["mla_sin"] = tables(32, 10000.0)
    strict, incl = (a < b).astype(f), (a <= b).astype(f)
    out["m512"] = np.concatenate([strict, incl, -strict, -incl], axis=1)
    lm = []
    for lev in range(7):
        n = 1 << lev
        lm.append(((a // (2 * n) == b // (2 * n)) & (a % (2 * n) < n) & (b % (2 * n) >= n)).astype(f))
    lm.append(-lm[0].T)
    out["lm"] = np.stack([np.concatenate(lm[:4], axis=1), np.concatenate(lm[4:], axis=1)])
    q, k = np.arange(T)[:, None], np.arange(T)[None, :]
    d = np.where(k // 64 <= q // 64, -np.abs(q - k).astype(f), NEG).astype(f)
    out["dist"] = np.concatenate([d[n * 128:n * 128 + 128, :(n + 1) * 128] for n in (0, 2, 3, 1)], axis=1)
    out["cmask"] = np.where(b // 64 <= a // 64, 0.0, NEG)
    ok = np.zeros((128, 4, 32), bool)
    ok[:, :, :31] = (np.arange(31) * 16 + 31)[None, None, :] <= (a + 128 * np.arange(4)[None, :])[:, :, None]
    out["cmp_mask"] = np.concatenate([np.where(ok, 0.0, NEG).reshape(128, 128), ok.reshape(128, 128)], axis=1)
    return {n: np.ascontiguousarray(v.astype(f)) for n, v in out.items()}


def _units(w, cols=None):
    import numpy as np

    if cols is not None:
        w = np.concatenate([w[:, c0:c1] for c0, c1 in cols], axis=1)
    k, m = w.shape
    return np.ascontiguousarray(w.reshape(k // 128, 128, m // 128, 128).transpose(2, 1, 0, 3)).reshape(
        m // 128, 128, k)


def _layout(x):
    import numpy as np

    f = np.float32
    x = {n: np.asarray(v) for n, v in x.items()}
    out = _constants()
    out["xT"] = np.ascontiguousarray(x["x"][0].T).reshape(8, 128, T)
    out["memT"] = np.ascontiguousarray(x["mem"][0].T).reshape(8, 128, 256)
    out["mem2T"] = np.ascontiguousarray(x["mem_2"][0].T).reshape(8, 128, 256)
    w = x["w_in"][0]
    o = 2176
    glog = np.concatenate([w[:, o + 512:o + 524], np.zeros((1024, 116), f)], axis=1)
    kc, vc, ks, vs, kw, vw = [(o + 524 + 64 * n, o + 588 + 64 * n) for n in range(6)]
    m0 = o + 908
    rest = [(0, 2048), (o, o + 256), (o + 256, o + 512), (m0, m0 + 256), kc, vc, ks, ks, kw, kw, vs, vw,
            (m0 + 256, m0 + 512), (2048, 2176)]
    out["w_in"] = np.concatenate([_units(glog), _units(w, rest)])
    out["w_mem_kv"] = _units(x["w_mem_kv"][0])
    out["w_out"] = _units(x["w_out"][0])
    e = x["ev_w_in_2"][0]
    out["ev_w_in"] = _units(e, [(0, 1984), (1920, 1984)])
    out["ev_w_out"] = _units(x["ev_w_out_2"][0])
    out["sb_w_in"], out["sb_w_out"] = _units(x["sb_w_in_2"][0]), _units(x["sb_w_out_2"][0])
    for n in range(2):
        out[f"wq{n}"], out[f"wkv{n}"], out[f"wo{n}"] = (_units(x[f"xa_{k}_2"][n]) for k in ("wq", "wkv", "wo"))
        out[f"w1{n}"] = _units(x["mlp_w1_2"][n])
        w2 = x["mlp_w2_2"][n]
        out[f"w2{n}"] = np.concatenate([_units(w2[q * 1024:q * 1024 + 1024]) for q in range(4)])
    uq = x["mla_w_uq_2"][0].reshape(2, 128, 4, 192)
    nope = uq[:, :, :, 0:128].transpose(2, 1, 0, 3)
    rope = uq[:, :, :, 128:192].reshape(2, 128, 2, 128).transpose(2, 1, 0, 3)
    tiles = np.concatenate([nope, rope, np.zeros((2, 128, 2, 128), f)])
    out["uq"] = np.ascontiguousarray(tiles.reshape(2, 4, 128, 256).transpose(0, 2, 1, 3)).reshape(2, 128, 1024)
    ukv = x["mla_w_ukv_2"][0].reshape(128, 4, 2, 128).transpose(0, 2, 1, 3)
    out["ukv"] = np.ascontiguousarray(ukv).reshape(1, 128, 1024)
    out["lora"] = np.concatenate([x["rwkv_w_up"][0], x["rwkv_a_up"][0]], axis=0)

    def w1(a):
        return a.reshape(32, 64, 64).transpose(1, 0, 2).reshape(64, 2048)

    out["cmp_w1"] = np.concatenate([w1(x["nsa_cmp_k_w1"][0]), w1(x["nsa_cmp_v_w1"][0])], axis=0)
    k2, v2 = x["nsa_cmp_k_w2"][0], x["nsa_cmp_v_w2"][0]
    out["cmp_w2"] = np.concatenate([k2, k2, v2], axis=1)

    def cols(a):
        return np.asarray(a).reshape(-1, 128).T

    z64 = np.zeros(64, f)
    pos = x["nsa_cmp_pos"][0].T
    p = {
        "norm_in_g": cols(x["norm_in_g"][0]), "mu": cols(x["rwkv_mu"][0]), "w0": cols(x["rwkv_w0"][0]),
        "a0h": cols(x["rwkv_a0"][0]), "k_k": cols(x["rwkv_k_k"][0]), "k_a": cols(x["rwkv_k_a"][0]),
        "r_k": cols(x["rwkv_r_k"][0]), "ln_w": cols(x["rwkv_ln_w"][0]), "ln_b": cols(x["rwkv_ln_b"][0]),
        "nsa_out_g": cols(x["nsa_out_g"][0]), "mem_norm_g": cols(x["mem_norm_g"][0]),
        "mem_out_g": cols(x["mem_out_g"][0]), "norm_final_g": cols(x["norm_final_g"]),
        "pos": np.concatenate([pos, pos], axis=0), "ev_norm": cols(x["ev_norm_2"][0]),
        "subln": cols(x["diff_subln_2"][0]), "g_cq": cols(x["mla_g_cq_2"][0]), "g_ckv": cols(x["mla_g_ckv_2"][0]),
        "od_norm": cols(x["od_norm_2"][0]), "final_norm": cols(x["final_norm_2"]),
        "lqk": np.stack([np.concatenate([x[n][0], z64]) for n in
                         ("diff_lq1_2", "diff_lq2_2", "diff_lk1_2", "diff_lk2_2")], axis=1),
        "gate_b": np.tile(x["nsa_gate_b"][0][None, :], (128, 1)),
        "eps6": np.full((128, 1), 1e-6), "gneps": np.full((128, 1), 64e-5), "one": np.ones((128, 1)),
        "half": np.full((128, 1), 0.5),
    }
    for n in range(2):
        p[f"xa_norm{n}"], p[f"xa_mem{n}"] = cols(x["xa_norm_2"][n]), cols(x["xa_mem_norm_2"][n])
        p[f"mlp_norm{n}"] = cols(x["mlp_norm_2"][n])
    out["pvec"] = np.concatenate([p[n].astype(f) for n, _ in PCOLS], axis=1)
    return {n: np.ascontiguousarray(v) for n, v in out.items()}


def kernel(**inputs):
    import numpy as np
    import concourse.bacc as bacc
    from concourse.bass_utils import run_bass_kernel_spmd as run

    arrays = _layout(inputs)
    nc = bacc.Bacc("TRN2", target_bir_lowering=False, num_devices=1)
    dram = {}
    for name, a in arrays.items():
        dram[name] = nc.dram_tensor("d_" + name, a.shape, mybir.dt.from_np(a.dtype), kind="ExternalInput").ap()
    dram["outT"] = nc.dram_tensor("d_outT", (8, 128, T), F32, kind="ExternalOutput").ap()
    build(nc, dram)
    r = run(nc, [{"d_" + name: a for name, a in arrays.items()}], core_ids=[0])
    got = r.results[0]["d_outT"]
    return np.ascontiguousarray(got.reshape(1024, T).T).reshape(1, T, 1024)
```
